# Optimizing a Trainium2 kernel written in Bass

```python
import jax, jax.numpy as jnp
from jax import lax
import numpy as np

D_MODEL = 2048
BATCH = 1
SEQ = 256
DEPTH = 2

CHUNK = 64
EPS = 1e-6
NEG_INF = -1e30

RET_HEADS = 8
RET_DK = D_MODEL // 16
RET_DV = D_MODEL // 16
RET_QK = RET_HEADS * RET_DK
RET_WIDTH = RET_HEADS * RET_DV
ROPE_BASE = 10000.0

POOL_WIDTH = D_MODEL - RET_WIDTH
POOL_WINDOWS = (2, 4, 8, 16)
POOL_GROUPS = len(POOL_WINDOWS)
POOL_GROUP_DIM = POOL_WIDTH // POOL_GROUPS

ATTN_HEADS = 32
KV_HEADS = 4
HEAD_DIM = D_MODEL // ATTN_HEADS
WINDOW = 128
WINDOW_CHUNKS = WINDOW // CHUNK

D_FF = 4 * D_MODEL

EVEN_IN = 2 * RET_QK + 2 * RET_WIDTH + POOL_WIDTH
ODD_IN = (ATTN_HEADS + 2 * KV_HEADS) * HEAD_DIM
N_EVEN = (DEPTH + 1) // 2
N_ODD = DEPTH // 2

kernel_name = "hybrid_retention_pool_swa_trunk"

def rms_norm(x, gain):
    xf = x.astype(jnp.float32)
    y = xf * lax.rsqrt(jnp.mean(xf * xf, axis=-1, keepdims=True) + EPS)
    return (y * gain.astype(jnp.float32)).astype(x.dtype)

def rotary(t, pos):
    half = t.shape[-1] // 2
    inv_freq = ROPE_BASE ** (-jnp.arange(half, dtype=jnp.float32) / half)
    ang = pos[:, None] * inv_freq[None, :]
    cos = jnp.cos(ang)[None, :, None, :]
    sin = jnp.sin(ang)[None, :, None, :]
    t1, t2 = t[..., :half], t[..., half:]
    return jnp.concatenate([t1 * cos - t2 * sin, t1 * sin + t2 * cos], axis=-1)

def retention(q, k, v):
    b, s, h, dk = q.shape
    dv = v.shape[-1]
    nc = s // CHUNK
    log_g = jnp.log(1.0 - 2.0 ** (-5.0 - jnp.arange(h, dtype=jnp.float32)))
    j = jnp.arange(CHUNK, dtype=jnp.float32)
    intra = jnp.exp(log_g[:, None, None] * jnp.abs(j[:, None] - j[None, :]))
    q_dec = jnp.exp(log_g[:, None] * (j + 1.0))
    k_dec = jnp.exp(log_g[:, None] * (CHUNK - 1.0 - j))
    c_dec = jnp.exp(log_g * CHUNK)

    def to_chunks(t):
        return t.reshape(b, nc, CHUNK, h, t.shape[-1]).transpose(1, 0, 3, 2, 4)

    qc, kc, vc = to_chunks(q), to_chunks(k * dk ** -0.5), to_chunks(v)

    def step(state, inp):
        qi, ki, vi = inp
        scores = jnp.einsum('bhid,bhjd->bhij', qi, ki) * intra
        o = (jnp.einsum('bhij,bhjv->bhiv', scores, vi)
             + jnp.einsum('bhid,bhdv->bhiv', qi * q_dec[None, :, :, None], state))
        state = (state * c_dec[None, :, None, None]
                 + jnp.einsum('bhjd,bhjv->bhdv', ki * k_dec[None, :, :, None], vi))
        return state, o

    init = jnp.zeros((b, h, dk, dv), jnp.float32)
    _, o = lax.scan(step, init, (qc, kc, vc))
    return o.transpose(1, 0, 3, 2, 4).reshape(b, s, h, dv)

def pool_mixer(p, pool_w, pool_scale):
    b, s, _ = p.shape
    pf = p.astype(jnp.float32)
    cs = jnp.concatenate([jnp.zeros((b, 1, POOL_WIDTH), jnp.float32),
                          jnp.cumsum(pf, axis=1)], axis=1)
    t1 = jnp.arange(1, s + 1)
    groups = []
    for gi, w in enumerate(POOL_WINDOWS):
        lo_c, hi_c = gi * POOL_GROUP_DIM, (gi + 1) * POOL_GROUP_DIM
        csg = cs[:, :, lo_c:hi_c]
        lo = jnp.maximum(t1 - w, 0)
        win_sum = csg[:, 1:] - jnp.take(csg, lo, axis=1)
        count = jnp.minimum(t1, w).astype(jnp.float32)
        groups.append(win_sum / count[None, :, None] - pf[:, :, lo_c:hi_c])
    diff = jnp.stack(groups, axis=2)
    y = jnp.einsum('bsgc,gcd->bsgd', diff, pool_w.astype(jnp.float32)).reshape(b, s, POOL_WIDTH)
    return (y * pool_scale.astype(jnp.float32)).astype(p.dtype)

def even_mixer(h, w_in, pool_w, pool_scale, w_out):
    b, s, _ = h.shape
    z = h @ w_in
    q, k, v, g, p = jnp.split(
        z, [RET_QK, 2 * RET_QK, 2 * RET_QK + RET_WIDTH, 2 * RET_QK + 2 * RET_WIDTH], axis=-1)
    pos = jnp.arange(s, dtype=jnp.float32)
    q = rotary(q.astype(jnp.float32).reshape(b, s, RET_HEADS, RET_DK), pos)
    k = rotary(k.astype(jnp.float32).reshape(b, s, RET_HEADS, RET_DK), pos)
    v = v.astype(jnp.float32).reshape(b, s, RET_HEADS, RET_DV)
    o = retention(q, k, v)
    mu = jnp.mean(o, axis=-1, keepdims=True)
    var = jnp.mean(jnp.square(o - mu), axis=-1, keepdims=True)
    o = (o - mu) * lax.rsqrt(var + EPS)
    ret = (o.reshape(b, s, RET_WIDTH) * jax.nn.silu(g.astype(jnp.float32))).astype(h.dtype)
    pool = pool_mixer(p, pool_w, pool_scale)
    return jnp.concatenate([ret, pool], axis=-1) @ w_out

def band(t, nc):
    parts = []
    for sh in range(WINDOW_CHUNKS - 1, -1, -1):
        parts.append(jnp.pad(t, ((0, 0), (sh, 0), (0, 0), (0, 0), (0, 0)))[:, :nc])
    return jnp.concatenate(parts, axis=2)

def odd_mixer(h, w_qkv, b_qkv, sinks, w_o, b_o):
    b, s, _ = h.shape
    nc = s // CHUNK
    r = ATTN_HEADS // KV_HEADS
    z = h @ w_qkv + b_qkv
    q, k, v = jnp.split(z, [ATTN_HEADS * HEAD_DIM, (ATTN_HEADS + KV_HEADS) * HEAD_DIM], axis=-1)
    qb = q.reshape(b, nc, CHUNK, KV_HEADS, r, HEAD_DIM)
    kw = band(k.reshape(b, nc, CHUNK, KV_HEADS, HEAD_DIM), nc)
    vw = band(v.reshape(b, nc, CHUNK, KV_HEADS, HEAD_DIM), nc)
    shifts = jnp.repeat(jnp.arange(WINDOW_CHUNKS - 1, -1, -1), CHUNK)
    valid = jnp.arange(nc)[:, None] >= shifts[None, :]
    scores = jnp.einsum('bncgrd,bnlgd->bgrncl', qb, kw,
                        preferred_element_type=jnp.float32) * HEAD_DIM ** -0.5
    scores = jnp.where(valid[:, None, :], scores, NEG_INF)
    sink = sinks.astype(jnp.float32).reshape(KV_HEADS, r)[None, :, :, None, None, None]
    m = jnp.maximum(jnp.max(scores, axis=-1, keepdims=True), sink)
    e = jnp.exp(scores - m)
    probs = e / (jnp.sum(e, axis=-1, keepdims=True) + jnp.exp(sink - m))
    o = jnp.einsum('bgrncl,bnlgd->bncgrd', probs.astype(vw.dtype), vw)
    return o.reshape(b, s, ATTN_HEADS * HEAD_DIM) @ w_o + b_o

def squared_relu_mlp(h, w1, w2):
    return jnp.square(jax.nn.relu(h @ w1)) @ w2

def setup_inputs(seed: int = 0) -> dict:
    key = jax.random.key(seed)
    ks = jax.random.split(key, 16)
    f32 = jnp.float32
    nrm = lambda k, shape, scale: (jax.random.normal(k, shape, f32) * scale)
    return {
        "x": nrm(ks[0], (BATCH, SEQ, D_MODEL), 1.0),
        "mix_norm": 1.0 + nrm(ks[1], (DEPTH, D_MODEL), 0.05),
        "mlp_norm": 1.0 + nrm(ks[2], (DEPTH, D_MODEL), 0.05),
        "w1": nrm(ks[3], (DEPTH, D_MODEL, D_FF), D_MODEL ** -0.5),
        "w2": nrm(ks[4], (DEPTH, D_FF, D_MODEL), D_FF ** -0.5),
        "rp_w_in": nrm(ks[5], (N_EVEN, D_MODEL, EVEN_IN), D_MODEL ** -0.5),
        "pool_w": nrm(ks[6], (N_EVEN, POOL_GROUPS, POOL_GROUP_DIM, POOL_GROUP_DIM), POOL_GROUP_DIM ** -0.5),
        "pool_scale": 1.0 + nrm(ks[7], (N_EVEN, POOL_WIDTH), 0.1),
        "rp_w_out": nrm(ks[8], (N_EVEN, D_MODEL, D_MODEL), D_MODEL ** -0.5),
        "attn_w_qkv": nrm(ks[9], (N_ODD, D_MODEL, ODD_IN), D_MODEL ** -0.5),
        "attn_b_qkv": nrm(ks[10], (N_ODD, ODD_IN), 0.02),
        "attn_sinks": nrm(ks[11], (N_ODD, ATTN_HEADS), 0.5),
        "attn_w_o": nrm(ks[12], (N_ODD, D_MODEL, D_MODEL), D_MODEL ** -0.5),
        "attn_b_o": nrm(ks[13], (N_ODD, D_MODEL), 0.02),
        "final_norm": 1.0 + nrm(ks[14], (D_MODEL,), 0.05),
    }

def reference(x, mix_norm, mlp_norm, w1, w2, rp_w_in, pool_w, pool_scale, rp_w_out,
              attn_w_qkv, attn_b_qkv, attn_sinks, attn_w_o, attn_b_o, final_norm):
    for i in range(DEPTH):
        h = rms_norm(x, mix_norm[i])
        if i % 2 == 0:
            e = i // 2
            y = even_mixer(h, rp_w_in[e], pool_w[e], pool_scale[e], rp_w_out[e])
        else:
            o = i // 2
            y = odd_mixer(h, attn_w_qkv[o], attn_b_qkv[o], attn_sinks[o], attn_w_o[o], attn_b_o[o])
        x = x + y
        h = rms_norm(x, mlp_norm[i])
        x = x + squared_relu_mlp(h, w1[i], w2[i])
    return rms_norm(x, final_norm)


_drawn_inputs = setup_inputs


def setup_inputs(seed=0):
    import zlib

    import numpy as np

    out = dict(_drawn_inputs(seed))
    spreads = {}
    factors = {'attn_b_qkv': 5.333, 'attn_sinks': 8.0, 'attn_b_o': 4.639}
    for name, (base, spread) in spreads.items():
        noise = np.random.default_rng([zlib.crc32(name.encode()), seed]).standard_normal(out[name].shape)
        drawn = base * np.exp(spread * noise) if base else spread * noise
        out[name] = __import__('jax').numpy.asarray(drawn.astype(out[name].dtype))
    for name, factor in factors.items():
        out[name] = (out[name] * factor).astype(out[name].dtype)
    return out
```

```python
from contextlib import ExitStack

import numpy as np

import concourse.bass as bass
from concourse import mybir

F32 = mybir.dt.float32
F32R = mybir.dt.float32r
ACT = mybir.ActivationFunctionType
ALU = mybir.AluOpType
AX_X = mybir.AxisListType.X

P = 128
D = 2048
S = 256
EPS = 1e-6
NEG_INF = -1e30
TT = S // P
KT = D // P
COLS = 512
SLABS = 8
SK = KT // SLABS
RING = 4
G4 = D // COLS

CHUNK = 64
HEADS, DK = 8, 128
POOL_WINDOWS = (2, 4, 8, 16)
PG = 256
TAIL = POOL_WINDOWS[-1]
KV, HD = 4, 64
D_FF = 4 * D

N_IN = 10
N_OUT = N_IN
N_MLP0 = N_OUT + G4
N_QKV = N_MLP0 + 2 * D_FF // COLS
N_WO = N_QKV + 5
N_MLP1 = N_WO + G4
N_END = N_MLP1 + 2 * D_FF // COLS
IN_COLS = [0, 1024, 2048, 512, 1536, 2560, 4096, 4608, 3072, 3584]
IN_POSTS = [1, 2, 2, 3, 4, 4, 4, 4, 5, 6]


def posts(n):
    if isinstance(n, int) and n < N_IN:
        return IN_POSTS[n]
    return n - 3


T_IN, H_IN = 8, 8
T_OUT, H_OUT = T_IN + 20, H_IN + 6
T_MLP0, H_MLP0 = T_OUT + 8, H_OUT + 8
T_QKV, H_QKV = T_MLP0 + 40, H_MLP0 + 40
T_WO, H_WO = T_QKV + 2 + 2 + 3 * 8, H_QKV + 2 + 3 * 2
T_MLP1, H_MLP1 = T_WO + 8 + 6, H_WO + 2 + 6
T_LAST, H_LAST = T_MLP1 + 2 + 38, H_MLP1 + 2 + 38


def build_program(nc, x, gains, w1, w2, w_in, pool_w, pool_gain, w_out, w_qkv, b_qkv, sink_cols, w_o, b_o,
                  final_gain, ident_c, rotary_c, decay_c, window_c, out):
    with ExitStack() as ctx:
        def sb(name, shape, dt=F32):
            return ctx.enter_context(nc.sbuf_tensor(name, shape, dt))

        def sem(name):
            return ctx.enter_context(nc.semaphore(name))

        raw = sb("raw", [P, SLABS, SK, COLS])
        w_hi = sb("w_hi", [P, RING, SK, COLS], F32R)
        w_lo = sb("w_lo", [P, RING, SK, COLS], F32R)
        xs = sb("xs", [P, TT, D])
        a_hi = sb("a_hi", [P, KT, S], F32R)
        a_lo = sb("a_lo", [P, KT, S], F32R)
        b_hi = sb("b_hi", [P, KT, S], F32R)
        b_lo = sb("b_lo", [P, KT, S], F32R)
        z = sb("z", [P, TT, COLS])
        zr = sb("zr", [P, TT, COLS])
        junk = sb("junk", [P, COLS])
        ident = sb("ident", [P, P])
        gain = sb("gain", [P, 4, KT])
        pool_g = sb("pool_g", [P, 8])
        sinks = sb("sinks", [P, 4 * KV])
        sumsq = sb("sumsq", [P, 5, TT * G4])
        meansq = sb("meansq", [P, 5, TT])
        rms = sb("rms", [P, 5, TT])
        rstd = sb("rstd", [P, 5, TT])
        stat = sb("stat", [P, 4, 8])
        soft = sb("soft", [P, 2, 4, 4])

        scratch = sb("scratch", [P, 12560])
        off = [0]

        def part(*shape):
            n = int(np.prod(shape))
            v = scratch[:, off[0]:off[0] + n]
            off[0] += n
            if len(shape) == 2:
                v = v.rearrange("p (a b) -> p a b", a=shape[0])
            if len(shape) == 3:
                v = v.rearrange("p (a b c) -> p a b c", a=shape[0], b=shape[1])
            return v

        r_qT = part(4, S)
        r_kT = part(4, S)
        r_o = part(TT, 1024)
        decay = part(HEADS, S)
        window = part(4, 2 * P + TAIL)
        pool_m = part(4, 2, PG)
        trig = part(TT, 2, DK // 2)
        r_p = part(2, S + P)
        diffT = part(4, S)
        rot = part(TT, 4, DK // 2)
        off[0] = 0
        bias = part(2560)
        bo = part(D)
        a_kT = part(KV, 3, P)
        v_pad = part(3 * KV, 3 * HD)
        a_qT = part(2 * 4, P)
        e_buf = part(4 * 4, P + 1)
        probT = part(2 * 4, P)
        fin_gain = bias[:, 0:D]

        acc = ctx.enter_context(nc.psum_tensor("acc", [P, 4 * COLS], F32))
        tb = [ctx.enter_context(nc.psum_tensor(f"tb{i}", [P, COLS], F32)) for i in range(2)]
        aux = [ctx.enter_context(nc.psum_tensor(f"aux{i}", [P, COLS], F32)) for i in range(2)]

        raw_in = [sem(f"raw_in{i}") for i in range(SLABS)]
        x_in = [sem(f"x_in{i}") for i in range(G4)]
        first_in = sem("first_in")
        const_in = sem("const_in")
        mixer_in = sem("mixer_in")
        final_in = sem("final_in")
        hi_done = sem("hi_done")
        lo_done = sem("lo_done")
        slab_done = sem("slab_done")
        evac_done = sem("evac_done")
        post_done = sem("post_done")
        t_full = sem("t_full")
        t_free = sem("t_free")
        op_hi = sem("op_hi")
        aux_full = sem("aux_full")
        aux_free = sem("aux_free")
        sumsq_done = sem("sumsq_done")
        mean_done = sem("mean_done")
        rms_done = sem("rms_done")
        rstd_done = sem("rstd_done")
        p_done = sem("p_done")
        p_used = sem("p_used")
        o_out = sem("o_out")
        o_centred = sem("o_centred")
        o_square = sem("o_square")
        o_var = sem("o_var")
        o_std = sem("o_std")
        e_in = sem("e_in")
        e_exp = sem("e_exp")
        e_prob = sem("e_prob")
        bo_added = sem("bo_added")
        out_ready0 = sem("out_ready0")
        out_ready1 = sem("out_ready1")
        out_sent = sem("out_sent")

        block = ctx.enter_context(nc.Block())

        def acc_of(n, t):
            return acc[:, bass.ds((n % 2) * (2 * COLS) + t * COLS, COLS)] if not isinstance(n, int) \
                else acc[:, (n % 2) * 2 * COLS + t * COLS:(n % 2) * 2 * COLS + (t + 1) * COLS]

        def cols(t, start, size):
            return t[:, :, start:start + size] if isinstance(start, int) else t[:, :, bass.ds(start, size)]

        def rows(t, start, size):
            return t[:, start:start + size, :] if isinstance(start, int) else t[:, bass.ds(start, size), :]

        @block.sync
        def _(sp):
            def load(n, w, row, col, turn=0):
                for s in range(SLABS):
                    if isinstance(n, int) and n == 0 and s % 2 == 0:
                        c = slice(s // 2 * COLS, (s // 2 + 1) * COLS)
                        sp.dma_start(xs[:, :, c], x[:, c].rearrange("(t p) c -> p t c", p=P)).then_inc(x_in[s // 2], 16)
                    if not isinstance(n, int) or n >= 1:
                        sp.wait_ge(lo_done, SLABS * (n - 1) + s + 1)
                    r = row + (s + turn) % SLABS * SK * P
                    rr = slice(r, r + SK * P) if isinstance(r, int) else bass.ds(r, SK * P)
                    cc = slice(col, col + COLS) if isinstance(col, int) else bass.ds(col, COLS)
                    sp.dma_start(raw[:, s, :, :],
                                 w[rr, cc].rearrange("(k p) c -> p k c", p=P)).then_inc(raw_in[s], 16)

            for n in range(N_IN):
                load(n, w_in, 0, IN_COLS[n])
            for g in range(G4):
                load(g + N_OUT, w_out, 0, g * COLS, turn=SLABS // 2)

            def mlp(layer, n0):
                with sp.Fori(0, 4) as q:
                    with sp.Fori(0, G4) as g:
                        load(q * 8 + g + n0, w1[layer], 0, q * D + g * COLS)
                    with sp.Fori(0, G4) as g:
                        load(q * 8 + g + (n0 + 4), w2[layer], q * D, g * COLS)

            mlp(0, N_MLP0)
            load(N_QKV, w_qkv, 0, D)
            for g in range(G4):
                load(g + (N_QKV + 1), w_qkv, 0, g * COLS)
            for g in range(G4):
                load(g + N_WO, w_o, 0, g * COLS)
            mlp(1, N_MLP1)
            for h in range(2):
                c = slice(h * (D // 2), (h + 1) * (D // 2))
                for t, ready in enumerate((out_ready0, out_ready1)):
                    sp.wait_ge(ready, h + 1)
                    sp.dma_start(out[t * P:(t + 1) * P, c], xs[:, t, c]).then_inc(out_sent, 16)
            sp.wait_ge(out_sent, 16 * 4)

        @block.gpsimd
        def _(pool):
            for dst, src in ((trig, rotary_c), (decay, decay_c),
                             (window, window_c), (pool_g[:], pool_gain), (sinks[:], sink_cols)):
                pool.dma_start(dst, src).then_inc(const_in, 16)
            pool.dma_start(pool_m, pool_w.rearrange("g (c p) d -> p g c d", p=P)).then_inc(const_in, 16)
            pool.wait_ge(slab_done, SLABS * (N_OUT + 1))
            pool.dma_start(bias, b_qkv.partition_broadcast(P)).then_inc(mixer_in, 16)
            pool.dma_start(bo, b_o.partition_broadcast(P)).then_inc(mixer_in, 16)
            pool.wait_ge(mixer_in, 32)
            pool.wait_ge(rstd_done, 3)
            pool.wait_ge(t_free, T_QKV + 2)
            for t in range(TT):
                last = pool.tensor_tensor(xs[:, t, :], xs[:, t, :], bo, ALU.add)
            last.then_inc(bo_added, 1)
            pool.wait_ge(post_done, posts(N_WO - 1))
            pool.dma_start(fin_gain, final_gain.partition_broadcast(P)).then_inc(final_in, 16)

        @block.tensor
        def _(pe):
            def group(n, x_hi, x_lo, after, before={}):
                for s in range(SLABS):
                    if s in before:
                        before[s]()
                    if s == 0 and (not isinstance(n, int) or n >= 2):
                        pe.wait_ge(evac_done, n - 1)
                    pe.wait_ge(lo_done, SLABS * n + s + 1)
                    for k in range(SK):
                        kt = s * SK + k
                        for t in range(TT):
                            tok = slice(t * P, (t + 1) * P)
                            hi, lo = w_hi[:, s % RING, k, :], w_lo[:, s % RING, k, :]
                            pe.matmul(acc_of(n, t), x_hi[:, kt, tok], hi, start=(kt == 0), stop=False)
                            pe.matmul(acc_of(n, t), x_hi[:, kt, tok], lo, start=False, stop=False)
                            mm = pe.matmul(acc_of(n, t), x_lo[:, kt, tok], hi, start=False, stop=(kt == KT - 1))
                    mm.then_inc(slab_done, 1)
                    if s in after:
                        after[s]()

            def transposes(T, src, ready, value):
                pe.wait_ge(ready, value)
                if not isinstance(T, int) or T > 0:
                    pe.wait_ge(t_free, T)
                for k in range(4):
                    for t in range(TT):
                        c = (k % 2) * S + t * P
                        mm = pe.transpose(tb[k // 2][:, c:c + P], src(k, t), ident[:])
                    if k % 2:
                        mm.then_inc(t_full, 1)

            def z_tile(k, t):
                return z[:, t, k * P:(k + 1) * P]

            def zr_tile(k, t):
                return zr[:, t, k * P:(k + 1) * P]

            def z_post(n, T):
                return {1: lambda: transposes(T, z_tile, post_done, posts(n - 1))}

            def x_quarter(j):
                return lambda: transposes(2 * j, lambda k, t: xs[:, t, (4 * j + k) * P:(4 * j + k + 1) * P], x_in[j], 16)

            def x_split(j):
                return lambda: pe.wait_ge(t_free, 2 * j + 2)

            pe.wait_ge(first_in, 32)
            x_quarter(0)()
            group(0, a_hi, a_lo, {2 * j - 2: x_quarter(j) for j in range(1, G4)}, {2 * j: x_split(j) for j in range(G4)})
            pe.wait_ge(const_in, 16 * 6)

            T, U, Hd = T_IN, 0, 0

            def rot_post(n, T):
                return {2: lambda: transposes(T, zr_tile, post_done, posts(n - 1))}

            def scores(h2, U, kq_ready):
                pe.wait_ge(t_free, kq_ready)
                if U:
                    pe.wait_ge(aux_free, U)
                for i in range(2):
                    h = 2 * h2 + i
                    pe.matmul(aux[i][:, 0:S], r_kT[:, h, 0:P], r_qT[:, h, :], start=True, stop=True)
                    pe.matmul(aux[i][:, S:S + P], r_kT[:, h, P:S], r_qT[:, h, P:S],
                              start=True, stop=True).then_inc(aux_full, 1)

            def values(h2, Hd):
                for i in range(2):
                    h = 2 * h2 + i
                    pe.wait_ge(p_done, Hd + i + 1)
                    v = [z[:, t, h * DK:(h + 1) * DK] for t in range(TT)]
                    o = [tb[t][:, h * DK:(h + 1) * DK] for t in range(TT)]
                    pe.matmul(o[0], r_p[:, i, 0:P], v[0], start=True, stop=True)
                    pe.matmul(o[1], r_p[:, i, P:S], v[0], start=True, stop=False)
                    mm = pe.matmul(o[1], r_p[:, i, S:S + P], v[1], start=False, stop=True)
                    if h < 3:
                        mm.then_inc(p_used, 1)
                    else:
                        mm.then_inc(t_full, 2)

            def retention(n, T, U, Hd):
                def first():
                    scores(0, U, T)

                def second():
                    pe.wait_ge(evac_done, n)
                    values(0, Hd)
                    scores(1, U + 2, T)

                def third():
                    values(1, Hd + 2)
                return {0: first, 2: second, 4: third}

            def pooling(n, T, U):
                def differences():
                    pe.wait_ge(evac_done, n)
                    if U:
                        pe.wait_ge(aux_free, U)
                    for c in range(4):
                        g = 2 * (n - 7) + c // 2
                        d = aux[c // 2][:, (c % 2) * S:(c % 2 + 1) * S]
                        z0, z1 = z_tile(c, 0), z_tile(c, 1)
                        pe.matmul(d[:, 0:P], z0, window[:, g, 0:P], start=True, stop=True)
                        pe.matmul(d[:, P:S], z1, window[:, g, P:2 * P], start=True, stop=True)
                        mm = pe.matmul(d[:, P:P + TAIL], z0, window[:, g, 2 * P:2 * P + TAIL],
                                       start=False, stop=True, skip_group_check=True)
                        if c % 2:
                            mm.then_inc(aux_full, 1)

                def mapped():
                    pe.wait_ge(aux_free, U + 2)
                    pe.wait_ge(t_free, T)
                    for a in range(2):
                        g = 2 * (n - 7) + a
                        for d in range(2):
                            for c in range(2):
                                mm = pe.matmul(tb[a][:, d * S:(d + 1) * S], pool_m[:, g, c, d * P:(d + 1) * P],
                                               diffT[:, 2 * a + c, :], start=(c == 0), stop=(c == 1))
                        mm.then_inc(t_full, 1)
                return {1: differences, 3: mapped}

            for n in range(1, N_IN):
                if n in (1, 2, 4, 5):
                    after = rot_post(n, T)
                    T += 2
                elif n in (3, 6):
                    after = retention(n, T, U, Hd)
                    T, U, Hd = T + 2, U + 4, Hd + 4
                elif n in (7, 8):
                    after = pooling(n, T, U)
                    T, U = T + 2, U + 2
                else:
                    after = z_post(n, T)
                    T += 2
                group(n, a_hi, a_lo, after)

            def need(T):
                return {6: lambda: pe.wait_ge(t_free, T)}

            def wide(n0, x_hi, x_lo, T, n_ops):
                with pe.Fori(0, G4 - 1) as i:
                    group(i + (n0 + 1), x_hi, x_lo, z_post(i + (n0 + 1), i * 2 + T) if n_ops else {})

            group(N_OUT, b_hi, b_lo, z_post(N_OUT, T), need(T + 2))
            wide(N_OUT, b_hi, b_lo, T_OUT, 2)

            def mlp(n0, T0):
                group(n0, a_hi, a_lo, z_post(n0, T0), need(T0 + 2))
                T1 = T0 + 2
                with pe.Fori(0, 3) as q:
                    with pe.Fori(0, 3) as i:
                        n = q * 8 + i + (n0 + 1)
                        group(n, a_hi, a_lo, z_post(n, q * 8 + i * 2 + T1))
                    n, T = q * 8 + (n0 + 4), q * 8 + (T1 + 6)
                    group(n, b_hi, b_lo, z_post(n, T), need(T + 2))
                    with pe.Fori(0, 3) as i:
                        group(q * 8 + i + (n0 + 5), b_hi, b_lo, {})
                    group(q * 8 + (n0 + 8), a_hi, a_lo, {})
                n1, T2 = n0 + 24, T1 + 24
                wide(n1, a_hi, a_lo, T2, 2)
                group(n1 + 4, b_hi, b_lo, z_post(n1 + 4, T2 + 6), need(T2 + 8))
                return n1 + 4, T2 + 8

            n1, T = mlp(N_MLP0, T_OUT + 6)
            wide(n1, b_hi, b_lo, T, 2)
            T += 6

            group(N_QKV, a_hi, a_lo, z_post(N_QKV, T), need(T + 2))
            T += 2

            def attention(n, g, T, U):
                def scores(two):
                    pe.wait_ge(aux_free, U + 2 * two)
                    for side in range(2):
                        rows_ = slice(side * HD, (side + 1) * HD)
                        for a in range(2):
                            for c in range(2):
                                chunk = 2 * two + c
                                win = (0, 0, 1, 2)[chunk]
                                o = (2 * a + c) * P
                                mm = pe.matmul(aux[side][:, o:o + P], a_qT[rows_, 4 * a + chunk, :],
                                               a_kT[rows_, g, win, :], start=True, stop=True)
                        mm.then_inc(aux_full, 1)

                def probs(two):
                    T1 = T + 2 + 3 * two
                    pe.wait_ge(t_free, T1)
                    for side in range(2):
                        pe.wait_ge(e_prob, U + 2 * two + side + 1 - U_ATT)
                        for i in range(4):
                            mm = pe.transpose(tb[side][:, i * P:(i + 1) * P], e_buf[:, 8 * two + 4 * side + i, 0:P], ident[:])
                        mm.then_inc(t_full, 1)

                def values(two):
                    T1 = T + 4 + 3 * two
                    pe.wait_ge(t_free, T1)
                    for c in range(2):
                        chunk = 2 * two + c
                        win = (0, 0, 1, 2)[chunk]
                        o = tb[0].rearrange("p (k t) -> p k t", k=4)[:, :, c * CHUNK:(c + 1) * CHUNK]
                        for side in range(2):
                            v = v_pad[:, win * KV + g, (1 - side) * HD:(1 - side) * HD + P]
                            pr = probT[:, 4 * side:4 * side + 4, :].rearrange("p (a c) r -> p a c r", c=2)[:, :, c, :]
                            mm = pe.matmul(o, v, pr, start=(side == 0), stop=(side == 1))
                    mm.then_inc(t_full, 1)

                def run(*steps):
                    return lambda: [f(i) for f, i in steps]

                def queries():
                    transposes(T, z_tile, post_done, posts(n - 1))

                def scores0():
                    pe.wait_ge(t_free, T + 2)
                    scores(0)
                if n == N_WO:
                    return {1: [queries], 2: [scores0], 3: [run((scores, 1))], 4: [run((probs, 0))],
                            5: [run((values, 0), (probs, 1), (values, 1))]}, {}
                return {1: [queries], 2: [scores0], 4: [run((scores, 1))], 6: [run((probs, 0))], 7: [run((values, 0))]}, \
                    {0: [run((probs, 1))], 1: [run((values, 1))]}

            group(N_QKV + 1, a_hi, a_lo, {2: lambda: transposes(T, zr_tile, post_done, posts(N_QKV))})
            T += 2
            U = U_ATT = 12
            late = {}
            for g in range(KV):
                n = N_QKV + 2 + g
                steps, later = attention(n, g, T, U)
                after = {s: (lambda fs: lambda: [f() for f in fs])(late.get(s, []) + steps.get(s, [])) for s in range(SLABS)}
                late = later
                if n < N_WO:
                    group(n, a_hi, a_lo, after)
                else:
                    group(n, b_hi, b_lo, after, need(T + 8))
                T, U = T + 8, U + 4

            wide(N_WO, b_hi, b_lo, T, 2)
            n1, T = mlp(N_MLP1, T + 6)
            wide(n1, b_hi, b_lo, T, 0)

        @block.scalar
        def _(act):
            def group(n, after):
                for s in range(SLABS):
                    act.wait_ge(raw_in[s], (n + 1) * 16)
                    if not isinstance(n, int) or n > 0 or s >= RING:
                        act.wait_ge(slab_done, SLABS * n + (s + 1 - RING))
                    act.copy(w_hi[:, s % RING, :, :], raw[:, s, :, :]).then_inc(hi_done, 1)
                    if s in after:
                        for f in after[s]:
                            f()

            def evac(n, func=ACT.Copy, norm=None):
                def run():
                    act.wait_ge(slab_done, SLABS * n)
                    if norm is not None:
                        act.wait_ge(rstd_done, norm + 1)
                    if not isinstance(n, int) or n >= 2:
                        act.wait_ge(post_done, posts(n - 2))
                    for t in range(TT):
                        s = 1.0 if norm is None else rstd[:, norm, t:t + 1]
                        last = act.activation(z[:, t, :], acc_of(n - 1, t), func, scale=s)
                    last.then_inc(evac_done, 1)
                return run

            def split(T, H, hi, kt, scales=None, halves=2):
                def run():
                    for b in range(halves):
                        act.wait_ge(t_full, T + b + 1)
                        if scales is None:
                            last = act.copy(rows(hi, kt + 2 * b, 2), tb[b].rearrange("p (k t) -> p k t", k=2))
                        else:
                            for k in range(2):
                                last = act.activation(rows(hi, kt + 2 * b + k, 1), tb[b][:, k * S:(k + 1) * S]
                                                      .rearrange("p (k t) -> p k t", k=1), ACT.Identity,
                                                      scale=scales(2 * b + k))
                        last.then_inc(op_hi, 1)
                return run

            def squares(norm, g, src, ready, value):
                def run():
                    for t in range(TT):
                        act.drain()
                        if t == 0:
                            act.wait_ge(ready, value)
                        s = t * G4 + g
                        s = sumsq[:, norm, s:s + 1] if isinstance(s, int) else sumsq[:, norm, bass.ds(s, 1)]
                        last = act.activation(junk[:], src(t), ACT.Square, accum_out=s)
                    act.drain().then_inc(sumsq_done, 1)
                return run

            def root(norm):
                def run():
                    act.wait_ge(mean_done, norm + 1)
                    act.activation(rms[:, norm, :], meansq[:, norm, :], ACT.Sqrt).then_inc(rms_done, 1)
                return run

            def gain_of(layer, g):
                def one(k):
                    c = g * 4 + k
                    return gain[:, layer, c:c + 1] if isinstance(c, int) else gain[:, layer, bass.ds(c, 1)]
                return one

            act.dma_start(ident[:], ident_c).then_inc(first_in, 16)
            act.dma_start(gain[:], gains).then_inc(first_in, 16)
            act.wait_ge(first_in, 32)
            split(0, 0, a_hi, 0, gain_of(0, 0))()
            T, H = T_IN, H_IN

            def copies(T, dst):
                def run():
                    for b in range(2):
                        act.wait_ge(t_full, T + b + 1)
                        act.copy(dst[:, 2 * b:2 * b + 2, :], tb[b].rearrange("p (k t) -> p k t", k=2)) \
                           .then_inc(t_free, 1)
                return run

            def results(T, half):
                def run():
                    act.wait_ge(t_full, T + 2)
                    for t in range(TT):
                        act.copy(r_o[:, t, half * COLS:(half + 1) * COLS], tb[t][:]).then_inc(t_free, 1)
                    act.drain().then_inc(o_out, 1)
                return run

            def deviations(half):
                def run():
                    act.wait_ge(o_centred, half + 1)
                    for t in range(TT):
                        last = act.activation(diffT[:, 2 * t:2 * t + 2, :].rearrange("p a b -> p (a b)"),
                                              r_o[:, t, half * COLS:(half + 1) * COLS], ACT.Square)
                    last.then_inc(o_square, 1)
                return run

            def o_root(half):
                def run():
                    act.wait_ge(o_var, half + 1)
                    act.activation(stat[:, 2, :], stat[:, 1, :], ACT.Sqrt).then_inc(o_std, 1)
                return run

            def differences(U):
                def run():
                    for b in range(2):
                        act.wait_ge(aux_full, U + b + 1)
                        act.copy(diffT[:, 2 * b:2 * b + 2, :], aux[b].rearrange("p (k t) -> p k t", k=2)) \
                           .then_inc(aux_free, 1)
                return run

            U = 0
            for n in range(N_IN):
                after = {}
                if n == 0:
                    after = {2 * j - 1: [split(2 * j, 2 * j, a_hi, 4 * j, gain_of(0, j))] for j in range(1, G4)}
                    for g, slot in enumerate((4, 6, 6, 7)):
                        after[slot] = after.get(slot, []) + [
                            squares(0, g, lambda t, g=g: xs[:, t, g * COLS:(g + 1) * COLS], x_in[g], 16)]
                elif n in (1, 2, 4, 5):
                    after = {2: [evac(n, ACT.Identity, 0)], 5: [copies(T, r_qT if n in (1, 4) else r_kT)]}
                    T += 2
                    if n == 1:
                        after[0] = [root(0)]
                    if n == 4:
                        after[3] = [deviations(0)]
                        after[6] = [o_root(0)]
                elif n in (3, 6):
                    after = {2: [evac(n, ACT.Identity, 0)], 7: [results(T, n // 6)]}
                    T, U = T + 2, U + 4
                elif n in (7, 8):
                    after = {2: [evac(n, ACT.Identity, 0)], 4: [differences(U)],
                             6: [split(T, H, b_hi, 4 * (n - 7), lambda k, n=n: pool_g[:, 4 * (n - 7) + k:4 * (n - 7) + k + 1])]}
                    if n == 7:
                        after[1] = [deviations(1)]
                        after[3] = [o_root(1)]
                    T, H, U = T + 2, H + 2, U + 2
                elif n == 9:
                    after = {2: [evac(n, ACT.Silu, 0)], 4: [split(T, H, b_hi, 8)]}
                    T, H = T + 2, H + 2
                group(n, after)

            group(N_OUT, {2: [evac(N_OUT, ACT.Silu, 0)], 4: [split(T, H, b_hi, 12)]})
            T, H = T + 2, H + 2

            def x_post(n, norm, layer, g, T, H):
                return {2: [evac(n)],
                        3: [squares(norm, g, lambda t: z[:, t, :], post_done, posts(n - 1))],
                        4: [split(T, H, a_hi, g * 4, gain_of(layer, g))]}

            def x_posts(n0, norm, layer, T, H):
                with act.Fori(0, 3) as i:
                    group(i + (n0 + 1), x_post(i + (n0 + 1), norm, layer, i, i * 2 + T, i * 2 + H))

            def last_x_post(n, norm, layer, T, H):
                after = x_post(n, norm, layer, 3, T, H)
                after[7] = [root(norm)]
                return after

            def f_post(n, norm, g, T, H):
                return {2: [evac(n, ACT.Relu, norm)], 4: [split(T, H, b_hi, g * 4)]}

            def mlp(n0, norm, layer, next_norm, T, H):
                group(n0, last_x_post(n0, norm, layer, T, H))
                T, H = T + 2, H + 2
                with act.Fori(0, 3) as q:
                    with act.Fori(0, 3) as i:
                        n = q * 8 + i + (n0 + 1)
                        group(n, f_post(n, norm, i, q * 8 + i * 2 + T, q * 8 + i * 2 + H))
                    n = q * 8 + (n0 + 4)
                    group(n, f_post(n, norm, 3, q * 8 + (T + 6), q * 8 + (H + 6)))
                    with act.Fori(0, 3) as i:
                        n = q * 8 + i + (n0 + 5)
                        group(n, {2: [evac(n)]})
                    n = q * 8 + (n0 + 8)
                    group(n, {2: [evac(n)]})
                n1, T, H = n0 + 24, T + 24, H + 24
                with act.Fori(0, 3) as i:
                    n = i + (n1 + 1)
                    group(n, f_post(n, norm, i, i * 2 + T, i * 2 + H))
                group(n1 + 4, f_post(n1 + 4, norm, 3, T + 6, H + 6))
                return n1 + 4, T + 8, H + 8

            x_posts(N_OUT, 1, 1, T, H)
            T, H = T + 6, H + 6
            n1, T, H = mlp(N_MLP0, 1, 1, 2, T, H)
            x_posts(n1, 2, 2, T, H)
            T, H = T + 6, H + 6

            group(N_QKV, last_x_post(N_QKV, 2, 2, T, H))
            T, H = T + 2, H + 2

            def keys(T):
                def run():
                    for b in range(2):
                        act.wait_ge(t_full, T + b + 1)
                        src = tb[b].rearrange("p (g t) -> p g t", g=2)
                        dst = a_kT[:, 2 * b:2 * b + 2, :, :]
                        act.copy(dst[:, :, 0, :], src[:, :, 0:P])
                        act.copy(dst[:, :, 2, :], src[:, :, P:S])
                        act.copy(dst[:, :, 1, 0:CHUNK], src[:, :, 2 * CHUNK:3 * CHUNK])
                        act.copy(dst[:, :, 1, CHUNK:P], src[:, :, CHUNK:2 * CHUNK])
                        act.drain().then_inc(t_free, 1)
                return run

            group(N_QKV + 1, {2: [evac(N_QKV + 1, ACT.Identity, 2)], 5: [keys(T)]})
            T += 2
            U = 0

            def attention(n, g, T, H, U):
                def queries():
                    for b in range(2):
                        act.wait_ge(t_full, T + b + 1)
                        act.mul(a_qT[:, 4 * b:4 * b + 4, :].rearrange("p c (k q) -> p k c q", k=2),
                                tb[b].rearrange("p (k c q) -> p k c q", k=2, c=4), HD ** -0.5).then_inc(t_free, 1)

                def exps(two):
                    for side in range(2):
                        act.wait_ge(e_in, U + 2 * two + side + 1)
                        e = e_buf[:, 8 * two + 4 * side:8 * two + 4 * side + 4, :]
                        act.activation(e, e, ACT.Exp).then_inc(e_exp, 1)

                def probs(two):
                    for side in range(2):
                        act.wait_ge(t_full, T + 2 + 3 * two + side + 1)
                        act.copy(probT[:, 4 * side:4 * side + 4, :], tb[side].rearrange("p (k t) -> p k t", k=4)) \
                           .then_inc(t_free, 1)

                def result(two):
                    act.wait_ge(t_full, T + 4 + 3 * two + 1)
                    act.copy(b_hi[:, 4 * g:4 * g + 4, two * P:(two + 1) * P],
                             tb[0].rearrange("p (k t) -> p k t", k=4)).then_inc(op_hi, 1)
                first, last = [lambda: exps(0)], [lambda: probs(1)]
                second, half = [lambda: exps(1)], [lambda: result(0)]
                if n == N_WO:
                    return {2: [evac(n, ACT.Identity, 2)], 3: [queries], 4: first, 5: second + [lambda: probs(0)],
                            6: half, 7: last + [lambda: result(1)]}, {}
                return {2: [evac(n, ACT.Identity, 2)], 3: [queries], 4: first, 6: second, 7: [lambda: probs(0)]}, \
                    {0: half, 1: last, 2: [lambda: result(1)]}

            late = {}
            for g in range(KV):
                n = N_QKV + 2 + g
                steps, later = attention(n, g, T, H, U)
                group(n, {s: late.get(s, []) + steps.get(s, []) for s in range(SLABS)})
                T, H, U, late = T + 8, H + 2, U + 4, later

            x_posts(N_WO, 3, 3, T, H)
            T, H = T + 6, H + 6
            n1, T, H = mlp(N_MLP1, 3, 3, 4, T, H)
            with act.Fori(0, 3) as i:
                n = i + (n1 + 1)
                group(n, {2: [evac(n)], 3: [squares(4, i, lambda t: z[:, t, :], post_done, posts(n - 1))]})
            evac(N_END)()
            squares(4, 3, lambda t: z[:, t, :], post_done, posts(N_END - 1))()
            root(4)()
            act.wait_ge(rstd_done, 5)
            for h in range(2):
                c = slice(h * (D // 2), (h + 1) * (D // 2))
                act.activation(xs[:, 1, c], xs[:, 1, c], ACT.Copy, scale=rstd[:, 4, 1:2]).then_inc(out_ready1, 1)

        @block.vector
        def _(dve):
            def group(n, after):
                for s in range(SLABS):
                    dve.wait_ge(hi_done, SLABS * n + (s + 1))
                    dve.tensor_tensor(w_lo[:, s % RING, :, :], raw[:, s, :, :],
                                      w_hi[:, s % RING, :, :].bitcast(F32), ALU.subtract).then_inc(lo_done, 1)
                    if s in after:
                        for f in after[s]:
                            f()

            def split(H, hi, lo, kt, scales=None):
                def run():
                    for b in range(2):
                        dve.wait_ge(op_hi, H + b + 1)
                        if scales is None:
                            last = dve.tensor_tensor(rows(lo, kt + 2 * b, 2), tb[b].rearrange("p (k t) -> p k t", k=2),
                                                     rows(hi, kt + 2 * b, 2).bitcast(F32), ALU.subtract)
                        else:
                            for k in range(2):
                                last = dve.scalar_tensor_tensor(
                                    out=rows(lo, kt + 2 * b + k, 1),
                                    in0=tb[b][:, k * S:(k + 1) * S].rearrange("p (k t) -> p k t", k=1),
                                    scalar=scales(2 * b + k), in1=rows(hi, kt + 2 * b + k, 1).bitcast(F32),
                                    op0=ALU.mult, op1=ALU.subtract)
                        last.then_inc(t_free, 1)
                return run

            def gain_of(layer, g):
                def one(k):
                    c = g * 4 + k
                    return gain[:, layer, c:c + 1] if isinstance(c, int) else gain[:, layer, bass.ds(c, 1)]
                return one

            def mean(norm):
                def run():
                    dve.wait_ge(sumsq_done, G4 * (norm + 1))
                    dve.tensor_reduce(meansq[:, norm, :], sumsq[:, norm, :].rearrange("p (t g) -> p t g", g=G4),
                                      AX_X, ALU.add)
                    dve.drain()
                    dve.tensor_scalar(meansq[:, norm, :], meansq[:, norm, :], 1.0 / D, EPS, ALU.mult, ALU.add) \
                       .then_inc(mean_done, 1)
                return run

            def inverse(norm):
                def run():
                    dve.wait_ge(rms_done, norm + 1)
                    dve.reciprocal(rstd[:, norm, :], rms[:, norm, :]).then_inc(rstd_done, 1)
                return run

            dve.wait_ge(first_in, 32)
            split(0, a_hi, a_lo, 0, gain_of(0, 0))()
            H = H_IN

            def rotate(n):
                def run():
                    dve.wait_ge(evac_done, n)
                    half = DK // 2
                    src = [z[:].rearrange("p t (h d) -> p t h d", h=4)[:, :, :, i * half:(i + 1) * half] for i in (0, 1)]
                    dst = [zr[:].rearrange("p t (h d) -> p t h d", h=4)[:, :, :, i * half:(i + 1) * half] for i in (0, 1)]
                    cos, sin = (trig[:, :, i, :].unsqueeze(2).broadcast_to([P, TT, 4, half]) for i in (0, 1))
                    dve.tensor_tensor(dst[0], src[0], cos, ALU.mult)
                    dve.tensor_tensor(rot, src[1], sin, ALU.mult)
                    dve.tensor_tensor(dst[1], src[0], sin, ALU.mult)
                    dve.drain()
                    dve.tensor_tensor(dst[0], dst[0], rot, ALU.subtract)
                    dve.drain()
                    dve.tensor_tensor(rot, src[1], cos, ALU.mult)
                    dve.drain()
                    dve.tensor_tensor(dst[1], dst[1], rot, ALU.add)
                    dve.drain().then_inc(post_done, 1)
                return run

            def decays(half, h2, U):
                def run():
                    for i in range(2):
                        h = 4 * half + 2 * h2 + i
                        dve.wait_ge(aux_full, U + i + 1)
                        if h2 == 1:
                            dve.wait_ge(p_used, 3 * half + i + 1)
                        dve.tensor_tensor(r_p[:, i, 0:S], aux[i][:, 0:S], decay[:, h, :], ALU.mult)
                        dve.tensor_tensor(r_p[:, i, S:S + P], aux[i][:, S:S + P], decay[:, h, 0:P], ALU.mult) \
                           .then_inc(aux_free, 1)
                        dve.drain().then_inc(p_done, 1)
                return run

            def heads_of(half):
                o = r_o[:, :, half * COLS:(half + 1) * COLS].rearrange("p t (h d) -> p t h d", h=4)
                return o

            def per_head(i):
                return stat[:, i, :].rearrange("p (t h) -> p t h", t=TT)

            def centre(half):
                def run():
                    o = heads_of(half)
                    dve.wait_ge(o_out, half + 1)
                    dve.tensor_reduce(per_head(0), o, AX_X, ALU.add)
                    dve.drain()
                    dve.tensor_scalar(stat[:, 0, :], stat[:, 0, :], 1.0 / DK, None, ALU.mult)
                    dve.drain()
                    dve.tensor_tensor(o, o, per_head(0).unsqueeze(3).broadcast_to([P, TT, 4, DK]), ALU.subtract) \
                       .then_inc(o_centred, 1)
                return run

            def variance(half):
                def run():
                    dve.wait_ge(o_square, half + 1)
                    sq = diffT.rearrange("p (t a) (h d) -> p t a h d", t=TT, h=2)
                    dve.tensor_reduce(stat[:, 1, :], diffT.rearrange("p a (h d) -> p (a h) d", h=2), AX_X, ALU.add)
                    dve.drain()
                    dve.tensor_scalar(stat[:, 1, :], stat[:, 1, :], 1.0 / DK, EPS, ALU.mult, ALU.add) \
                       .then_inc(o_var, 1)
                return run

            def scale(half):
                def run():
                    o = heads_of(half)
                    dve.wait_ge(o_std, half + 1)
                    dve.reciprocal(stat[:, 3, :], stat[:, 2, :])
                    dve.drain()
                    dve.tensor_tensor(o, o, per_head(3).unsqueeze(3).broadcast_to([P, TT, 4, DK]), ALU.mult)
                return run

            def gate(n, half):
                def run():
                    dve.wait_ge(evac_done, n)
                    dve.drain()
                    dve.tensor_tensor(z[:], z[:], r_o[:, :, half * COLS:(half + 1) * COLS], ALU.mult) \
                       .then_inc(post_done, 1)
                return run

            U = 0
            for n in range(N_IN):
                after = {}
                if n == 0:
                    after = {2 * j - 1: [split(2 * j, a_hi, a_lo, 4 * j, gain_of(0, j))] for j in range(1, G4)}
                elif n in (1, 2, 4, 5):
                    after = {2: [rotate(n)]}
                    if n == 1:
                        after[0] = [mean(0), lambda: dve.wait_ge(const_in, 16 * 6)]
                        after[1] = [inverse(0)]
                    if n == 4:
                        after[1] = [centre(0)]
                        after[4] = [variance(0)]
                        after[7] = [scale(0)]
                elif n in (3, 6):
                    after = {3: [decays(n // 6, 0, U)], 5: [decays(n // 6, 1, U + 2)]}
                    U += 4
                elif n in (7, 8):
                    after = {6: [split(H, b_hi, b_lo, 4 * (n - 7), lambda k, n=n: pool_g[:, 4 * (n - 7) + k:4 * (n - 7) + k + 1])]}
                    if n == 7:
                        after[0] = [centre(1)]
                        after[2] = [variance(1)]
                        after[4] = [scale(1)]
                    H += 2
                elif n == 9:
                    after = {2: [gate(n, 0)], 4: [split(H, b_hi, b_lo, 8)]}
                    H += 2
                group(n, after)

            group(N_OUT, {2: [gate(N_OUT, 1)], 4: [split(H, b_hi, b_lo, 12)]})
            H += 2

            def x_add(n, g, keep):
                def run():
                    dve.wait_ge(evac_done, n)
                    xg = cols(xs, g * COLS, COLS)
                    add = dve.tensor_tensor(xg, xg, z[:], ALU.add)
                    if not keep:
                        add.then_inc(post_done, 1)
                        return
                    dve.drain()
                    dve.tensor_copy(z[:], xg).then_inc(post_done, 1)
                return run

            def x_post(n, layer, g, H):
                return {2: [x_add(n, g, True)], 4: [split(H, a_hi, a_lo, g * 4, gain_of(layer, g))]}

            def x_posts(n0, layer, H):
                with dve.Fori(0, 3) as i:
                    group(i + (n0 + 1), x_post(i + (n0 + 1), layer, i, i * 2 + H))

            def last_x_post(n, norm, layer, H):
                after = x_post(n, layer, 3, H)
                after[6] = [mean(norm)]
                after[7] = [inverse(norm)]
                return after

            def f_post(n, g, H):
                def square():
                    dve.wait_ge(evac_done, n)
                    dve.tensor_tensor(z[:], z[:], z[:], ALU.mult).then_inc(post_done, 1)
                return {2: [square], 4: [split(H, b_hi, b_lo, g * 4)]}

            def mlp(n0, norm, layer, H):
                group(n0, last_x_post(n0, norm, layer, H))
                H += 2
                with dve.Fori(0, 3) as q:
                    with dve.Fori(0, 3) as i:
                        n = q * 8 + i + (n0 + 1)
                        group(n, f_post(n, i, q * 8 + i * 2 + H))
                    n = q * 8 + (n0 + 4)
                    group(n, f_post(n, 3, q * 8 + (H + 6)))
                    with dve.Fori(0, 3) as i:
                        n = q * 8 + i + (n0 + 5)
                        group(n, {2: [x_add(n, i, False)]})
                    n = q * 8 + (n0 + 8)
                    group(n, {2: [x_add(n, 3, False)]})
                n1, H = n0 + 24, H + 24
                with dve.Fori(0, 3) as i:
                    n = i + (n1 + 1)
                    group(n, f_post(n, i, i * 2 + H))
                group(n1 + 4, f_post(n1 + 4, 3, H + 6))
                return n1 + 4, H + 8

            x_posts(N_OUT, 1, H)
            H += 6
            n1, H = mlp(N_MLP0, 1, 1, H)
            x_posts(n1, 2, H)
            H += 6

            def zeros():
                dve.memset(v_pad, 0.0)
            after = last_x_post(N_QKV, 2, 2, H)
            after[1] = [zeros]
            group(N_QKV, after)
            H += 2

            def keys_values():
                dve.wait_ge(evac_done, N_QKV + 1)
                dve.wait_ge(mixer_in, 32)
                kd = zr[:].rearrange("p t (g u d) -> p t g u d", g=KV, u=2)
                for t in range(TT):
                    k = z[:, t, 0:KV * HD].rearrange("p (g d) -> p g d", g=KV)
                    for u in range(2):
                        dve.tensor_tensor(kd[:, t, :, u, :], k, bias[:, D:D + 256].rearrange("p (g d) -> p g d", g=KV),
                                          ALU.add)
                vb = bias[:, D + 256:D + 512].rearrange("p (g d) -> p g d", g=KV)
                for win, t, lo, hi in ((0, 0, 0, P), (2, 1, 0, P), (1, 1, 0, CHUNK), (1, 0, CHUNK, P)):
                    v = z[lo:hi, t, 256:512].rearrange("p (g d) -> p g d", g=KV)
                    last = dve.tensor_tensor(v_pad[lo:hi, win * KV:(win + 1) * KV, HD:2 * HD], v, vb[lo:hi], ALU.add)
                dve.drain().then_inc(post_done, 1)

            group(N_QKV + 1, {2: [keys_values]})

            def attention(n, g, H, U):
                def queries():
                    dve.wait_ge(evac_done, n)
                    b = bias[:, g * COLS:(g + 1) * COLS].unsqueeze(1).broadcast_to([P, TT, COLS])
                    dve.tensor_tensor(z[:], z[:], b, ALU.add).then_inc(post_done, 1)

                def softmax(two):
                    for side in range(2):
                        u = U + 2 * two + side
                        s4 = aux[side].rearrange("p (k l) -> p k l", k=4)
                        e = e_buf[:, 8 * two + 4 * side:8 * two + 4 * side + 4, :]
                        sink = sinks[:, 4 * g + 2 * side:4 * g + 2 * side + 2].unsqueeze(2).broadcast_to([P, 2, 2])
                        top, m = soft[:, side, 0, :], soft[:, side, 1, :]
                        m22 = m.rearrange("p (a c) -> p a c", a=2)
                        dve.wait_ge(aux_full, 12 + u + 1)
                        if two == 0:
                            dve.memset(s4.rearrange("p (a c) l -> p a c l", c=2)[:, :, 0, CHUNK:P], NEG_INF)
                            dve.drain()
                        dve.tensor_reduce(top, s4, AX_X, ALU.max)
                        dve.drain()
                        dve.tensor_tensor(m22, top.rearrange("p (a c) -> p a c", a=2), sink, ALU.max)
                        dve.drain()
                        dve.tensor_tensor(e[:, :, P:P + 1].rearrange("p (a c) l -> p a (c l)", a=2), sink, m22, ALU.subtract)
                        dve.tensor_tensor(e[:, :, 0:P], s4, m.unsqueeze(2).broadcast_to([P, 4, P]), ALU.subtract) \
                           .then_inc(aux_free, 1)
                        dve.drain().then_inc(e_in, 1)
                    for side in range(2):
                        u = U + 2 * two + side
                        e = e_buf[:, 8 * two + 4 * side:8 * two + 4 * side + 4, :]
                        total, inv = soft[:, side, 2, :], soft[:, side, 3, :]
                        dve.wait_ge(e_exp, u + 1)
                        dve.tensor_reduce(total, e, AX_X, ALU.add)
                        dve.drain()
                        dve.reciprocal(inv, total)
                        dve.drain()
                        dve.tensor_tensor(e[:, :, 0:P], e[:, :, 0:P], inv.unsqueeze(2).broadcast_to([P, 4, P]),
                                          ALU.mult).then_inc(e_prob, 1)

                def result(two):
                    dve.wait_ge(op_hi, H + two + 1)
                    tok = slice(two * P, (two + 1) * P)
                    dve.tensor_tensor(b_lo[:, 4 * g:4 * g + 4, tok], tb[0].rearrange("p (k t) -> p k t", k=4),
                                      b_hi[:, 4 * g:4 * g + 4, tok].bitcast(F32), ALU.subtract).then_inc(t_free, 1)
                if n == N_WO:
                    return {2: [queries], 4: [lambda: softmax(0)], 5: [lambda: softmax(1)],
                            6: [lambda: result(0)], 7: [lambda: result(1)]}, {}
                return {2: [queries], 4: [lambda: softmax(0)], 6: [lambda: softmax(1)]}, \
                    {0: [lambda: result(0)], 2: [lambda: result(1)]}

            U, late = 0, {}
            for g in range(KV):
                n = N_QKV + 2 + g
                steps, later = attention(n, g, H, U)
                group(n, {s: late.get(s, []) + steps.get(s, []) for s in range(SLABS)})
                H, U, late = H + 2, U + 4, later

            dve.wait_ge(bo_added, 1)
            x_posts(N_WO, 3, H)
            H += 6
            n1, H = mlp(N_MLP1, 3, 3, H)
            dve.wait_ge(final_in, 16)

            def x_final(n, g):
                def run():
                    dve.wait_ge(evac_done, n)
                    xg = cols(xs, g * COLS, COLS)
                    dve.tensor_tensor(z[:], z[:], xg, ALU.add).then_inc(post_done, 1)
                    dve.wait_ge(post_done, posts(n - 1))
                    fg = fin_gain[:, bass.ds(g * COLS, COLS)] if not isinstance(g, int) else fin_gain[:, g * COLS:]
                    dve.tensor_tensor(xg, z[:], fg.unsqueeze(1).broadcast_to([P, TT, COLS]), ALU.mult)
                return run

            with dve.Fori(0, 3) as i:
                group(i + (n1 + 1), {2: [x_final(i + (n1 + 1), i)]})
            x_final(N_END, 3)()
            mean(4)()
            inverse(4)()
            dve.drain()
            for h in range(2):
                c = slice(h * (D // 2), (h + 1) * (D // 2))
                dve.tensor_scalar(xs[:, 0, c], xs[:, 0, c], rstd[:, 4, 0:1], None, ALU.mult).then_inc(out_ready0, 1)


def rotary_table():
    half = DK // 2
    inv_freq = (np.float32(10000.0) ** (-np.arange(half, dtype=np.float32) / np.float32(half))).astype(np.float32)
    ang = np.arange(S, dtype=np.float32)[:, None] * inv_freq[None, :]
    t = np.stack([np.cos(ang), np.sin(ang)], axis=1)
    return np.ascontiguousarray(t.reshape(TT, P, 2, half).transpose(1, 0, 2, 3).astype(np.float32))


def decay_table():
    g = 1.0 - 2.0 ** (-5.0 - np.arange(HEADS))[:, None, None]
    j, i = np.arange(P)[:, None], np.arange(P)[None, :]
    same = np.where(j // CHUNK <= i // CHUNK, g ** np.abs(i - j), 0.0)
    later = g ** (P + i - j)
    t = np.concatenate([same, later], axis=2) * DK ** -0.5
    return np.ascontiguousarray(t.transpose(1, 0, 2).astype(np.float32))


def window_table():
    s, t = np.arange(S)[:, None], np.arange(S)[None, :]
    out = np.zeros((P, len(POOL_WINDOWS), 2 * P + TAIL))
    for g, w in enumerate(POOL_WINDOWS):
        m = np.where((s <= t) & (s > t - w), 1.0 / np.minimum(t + 1, w), 0.0) - (s == t)
        out[:, g, 0:P], out[:, g, P:2 * P], out[:, g, 2 * P:] = m[:P, :P], m[P:, P:], m[:P, P:P + TAIL]
    return out.astype(np.float32)


def kernel(x, mix_norm, mlp_norm, w1, w2, rp_w_in, pool_w, pool_scale, rp_w_out,
           attn_w_qkv, attn_b_qkv, attn_sinks, attn_w_o, attn_b_o, final_norm):
    import concourse.bacc as _bacc
    from concourse.bass_utils import run_bass_kernel_spmd as _run

    a = {k: np.asarray(v) for k, v in dict(
        x=x, mix_norm=mix_norm, mlp_norm=mlp_norm, w1=w1, w2=w2, w_in=rp_w_in, pool_w=pool_w,
        pool_scale=pool_scale, w_out=rp_w_out, w_qkv=attn_w_qkv, b_qkv=attn_b_qkv, sinks=attn_sinks,
        w_o=attn_w_o, b_o=attn_b_o, final=final_norm).items()}
    norms = np.stack([a["mix_norm"][0], a["mlp_norm"][0], a["mix_norm"][1], a["mlp_norm"][1]])
    gains = np.ascontiguousarray(norms.reshape(4, KT, P).transpose(2, 0, 1))
    pool_gain = np.ascontiguousarray(a["pool_scale"][0].reshape(8, P).T)
    s = a["sinks"][0].reshape(KV, 2, 2, 2).transpose(2, 0, 3, 1).reshape(2, 4 * KV)
    sink_cols = np.ascontiguousarray(np.repeat(s, HD, axis=0))
    arrays = {
        "x": a["x"][0], "gains": gains, "w1": a["w1"], "w2": a["w2"], "w_in": a["w_in"][0],
        "pool_w": a["pool_w"][0], "pool_gain": pool_gain, "w_out": a["w_out"][0], "w_qkv": a["w_qkv"][0],
        "b_qkv": a["b_qkv"][0], "sink_cols": sink_cols, "w_o": a["w_o"][0], "b_o": a["b_o"][0],
        "final_gain": a["final"], "ident_c": np.eye(P, dtype=np.float32), "rotary_c": rotary_table(),
        "decay_c": decay_table(), "window_c": window_table(),
    }
    arrays = {k: np.ascontiguousarray(v) for k, v in arrays.items()}
    nc = _bacc.Bacc("TRN2", target_bir_lowering=False, num_devices=1)
    args = {k: nc.dram_tensor(f"in_{k}", v.shape, mybir.dt.from_np(v.dtype), kind="ExternalInput").ap()
            for k, v in arrays.items()}
    out = nc.dram_tensor("out_0", (S, D), F32, kind="ExternalOutput").ap()
    build_program(nc, out=out, **args)
    r = _run(nc, [{f"in_{k}": v for k, v in arrays.items()}], core_ids=[0])
    return r.results[0]["out_0"].reshape(1, S, D)
```

```python
from contextlib import ExitStack

import numpy as np

import concourse.bass as bass
from concourse import mybir

F32 = mybir.dt.float32
F32R = mybir.dt.float32r
ACT = mybir.ActivationFunctionType
ALU = mybir.AluOpType
AX_X = mybir.AxisListType.X

P = 128
D = 2048
S = 256
EPS = 1e-6
NEG_INF = -1e30
TT = S // P
KT = D // P
COLS = 512
SLABS = 8
SK = KT // SLABS
RING = 4
G4 = D // COLS

CHUNK = 64
HEADS, DK = 8, 128
POOL_WINDOWS = (2, 4, 8, 16)
PG = 256
TAIL = POOL_WINDOWS[-1]
KV, HD = 4, 64
D_FF = 4 * D

N_IN = 10
N_OUT = N_IN
N_MLP0 = N_OUT + G4
N_QKV = N_MLP0 + 2 * D_FF // COLS
N_WO = N_QKV + 5
N_MLP1 = N_WO + G4
N_END = N_MLP1 + 2 * D_FF // COLS
IN_COLS = [0, 1024, 2048, 512, 1536, 2560, 4096, 4608, 3072, 3584]
IN_POSTS = [1, 2, 2, 3, 4, 4, 4, 4, 5, 6]

WO_ORDER = [(N_WO, s) for s in range(6)] + [(N_WO + 1, s) for s in range(4)] \
    + [(N_WO, s) for s in range(6, 8)] + [(N_WO + 1, s) for s in range(4, 8)]
WO_DONE = WO_ORDER.index((N_WO, 7)) + 1 - SLABS


def posts(n):
    if isinstance(n, int) and n < N_IN:
        return IN_POSTS[n]
    return n - 3


T_IN, H_IN = 8, 8
T_QKV = T_IN + 2 * (N_IN - 1) + 2 * G4 + 2 * D_FF // COLS + 2 * G4
U_ATT = 12


def build_program(nc, x, ident_gains, w1, w2, w_in, pool_w, pool_gain, w_out, w_qkv, b_qkv, sink_cols, w_o, b_o,
                  final_gain, rotary_c, decay_c, window_c, out):
    with ExitStack() as ctx:
        def sb(name, shape, dt=F32):
            return ctx.enter_context(nc.sbuf_tensor(name, shape, dt))

        def sem(name):
            return ctx.enter_context(nc.semaphore(name))

        raw = sb("raw", [P, SLABS, SK, COLS])
        w_hi = sb("w_hi", [P, RING, SK, COLS], F32R)
        w_lo = sb("w_lo", [P, RING, SK, COLS], F32R)
        xs = sb("xs", [P, TT, D])
        a_hi = sb("a_hi", [P, KT, S], F32R)
        a_lo = sb("a_lo", [P, KT, S], F32R)
        b_hi = sb("b_hi", [P, KT, S], F32R)
        b_lo = sb("b_lo", [P, KT, S], F32R)
        z = sb("z", [P, TT, COLS])
        zr = sb("zr", [P, TT, COLS])
        junk = sb("junk", [P, COLS])
        ident_gain = sb("ident_gain", [P, P + 4 * KT])
        ident = ident_gain[:, 0:P]
        gain = ident_gain[:, P:].rearrange("p (n k) -> p n k", n=4)
        pool_g = sb("pool_g", [P, 8])
        sinks = sb("sinks", [P, 4 * KV])
        sumsq = sb("sumsq", [P, 5, TT * G4])
        meansq = sb("meansq", [P, 5, TT])
        rms = sb("rms", [P, 5, TT])
        rstd = sb("rstd", [P, 5, TT])
        stat = sb("stat", [P, 4, 8])
        minus_sinks = sb("minus_sinks", [P, 4 * KV])
        soft = sb("soft", [P, 2, 5, 8])

        scratch = sb("scratch", [P, 12560])
        off = [0]

        def part(*shape):
            n = int(np.prod(shape))
            v = scratch[:, off[0]:off[0] + n]
            off[0] += n
            if len(shape) == 2:
                v = v.rearrange("p (a b) -> p a b", a=shape[0])
            if len(shape) == 3:
                v = v.rearrange("p (a b c) -> p a b c", a=shape[0], b=shape[1])
            return v

        r_qT = part(4, S)
        r_kT = part(4, S)
        r_o = part(TT, 1024)
        decay = part(HEADS, S)
        window = part(4, 2 * P + TAIL)
        pool_m = part(4, 2, PG)
        trig = part(TT, 2, DK // 2)
        r_p = part(2, S + P)
        diffT = part(4, S)
        rot = part(TT, 4, DK // 2)
        off[0] = 0
        bias = part(2560)
        bo = part(D)
        a_kT = part(KV, 3, P)
        v_pad = part(3 * KV, 3 * HD)
        a_qT = part(2 * 4, P)
        e_buf = part(4 * 4, P)
        probT = part(2 * 4, P)
        fin_gain = bias[:, 0:D]

        acc = ctx.enter_context(nc.psum_tensor("acc", [P, 4 * COLS], F32))
        tb = [ctx.enter_context(nc.psum_tensor(f"tb{i}", [P, COLS], F32)) for i in range(2)]
        aux_both = ctx.enter_context(nc.psum_tensor("aux_both", [P, 2 * COLS], F32))
        aux = [aux_both[:, i * COLS:(i + 1) * COLS] for i in range(2)]

        raw_in = [sem(f"raw_in{i}") for i in range(SLABS)]
        x_in = [sem(f"x_in{i}") for i in range(G4)]
        first_in = sem("first_in")
        warm = sem("warm")
        const_in = sem("const_in")
        mixer_in = sem("mixer_in")
        final_in = sem("final_in")
        hi_done = sem("hi_done")
        lo_done = sem("lo_done")
        slab_done = sem("slab_done")
        evac_done = sem("evac_done")
        post_done = sem("post_done")
        t_full = sem("t_full")
        t_free = sem("t_free")
        op_hi = sem("op_hi")
        aux_full = sem("aux_full")
        aux_free = sem("aux_free")
        sumsq_done = sem("sumsq_done")
        mean_done = sem("mean_done")
        rms_done = sem("rms_done")
        rstd_done = sem("rstd_done")
        p_done = sem("p_done")
        p_used = sem("p_used")
        o_out = sem("o_out")
        o_centred = sem("o_centred")
        o_square = sem("o_square")
        o_var = sem("o_var")
        o_std = sem("o_std")
        max_done = sem("max_done")
        exp_done = sem("exp_done")
        prob_done = sem("prob_done")
        bo_added = sem("bo_added")
        tile_done = sem("tile_done")
        out_dve = sem("out_dve")
        out_act = sem("out_act")
        out_sent = sem("out_sent")

        block = ctx.enter_context(nc.Block())

        def acc_of(n, t):
            return acc[:, bass.ds((n % 2) * (2 * COLS) + t * COLS, COLS)] if not isinstance(n, int) \
                else acc[:, (n % 2) * 2 * COLS + t * COLS:(n % 2) * 2 * COLS + (t + 1) * COLS]

        def cols(t, start, size):
            return t[:, :, start:start + size] if isinstance(start, int) else t[:, :, bass.ds(start, size)]

        def rows(t, start, size):
            return t[:, start:start + size, :] if isinstance(start, int) else t[:, bass.ds(start, size), :]

        def gain_of(norm, g):
            def one(k):
                c = g * 4 + k
                return gain[:, norm, c:c + 1] if isinstance(c, int) else gain[:, norm, bass.ds(c, 1)]
            return one

        def pool_gain_of(half):
            return lambda k: pool_g[:, 4 * half + k:4 * half + k + 1]

        @block.sync
        def _(sp):
            def load(n, w, row, col, turn=0, order=None):
                for s in range(SLABS):
                    if order is not None:
                        g, turn = order[s][0] - N_WO, order[s][1] - s
                        col = g * COLS
                    if isinstance(n, int) and n == 0 and s % 2 == 0:
                        c = slice(s // 2 * COLS, (s // 2 + 1) * COLS)
                        sp.dma_start(xs[:, :, c], x[:, c].rearrange("(t p) c -> p t c", p=P)).then_inc(x_in[s // 2], 16)
                    if not isinstance(n, int) or n >= 1:
                        sp.wait_ge(lo_done, SLABS * (n - 1) + s + 1)
                    r = row + (s + turn) % SLABS * SK * P
                    rr = slice(r, r + SK * P) if isinstance(r, int) else bass.ds(r, SK * P)
                    cc = slice(col, col + COLS) if isinstance(col, int) else bass.ds(col, COLS)
                    sp.dma_start(raw[:, s, :, :],
                                 w[rr, cc].rearrange("(k p) c -> p k c", p=P)).then_inc(raw_in[s], 16)

            for n in range(N_IN):
                load(n, w_in, 0, IN_COLS[n])
            for g in range(G4):
                load(g + N_OUT, w_out, 0, g * COLS, turn=SLABS // 2)

            def mlp(layer, n0):
                with sp.Fori(0, 4) as q:
                    with sp.Fori(0, G4) as g:
                        load(q * 8 + g + n0, w1[layer], 0, q * D + g * COLS)
                    with sp.Fori(0, G4) as g:
                        load(q * 8 + g + (n0 + 4), w2[layer], q * D, g * COLS)

            mlp(0, N_MLP0)
            load(N_QKV, w_qkv, 0, D)
            for g in range(G4):
                load(g + (N_QKV + 1), w_qkv, 0, g * COLS)
            for g in range(2):
                load(g + N_WO, w_o, 0, 0, order=WO_ORDER[g * SLABS:(g + 1) * SLABS])
            for g in range(2, G4):
                load(g + N_WO, w_o, 0, g * COLS)
            mlp(1, N_MLP1)
            for t in range(TT):
                for i, (ready, g) in enumerate(((out_dve, 0), (out_act, 1), (out_dve, 3), (out_act, 2))):
                    sp.wait_ge(ready, 2 * t + i // 2 + 1)
                    c = slice(g * COLS, (g + 1) * COLS)
                    sp.dma_start(out[t * P:(t + 1) * P, c], xs[:, t, c]).then_inc(out_sent, 16)
            sp.wait_ge(out_sent, 16 * TT * G4)

        @block.gpsimd
        def _(pool):
            pool.wait_ge(raw_in[3], 16)
            for dst, src in ((trig, rotary_c), (decay, decay_c),
                             (window, window_c), (pool_g[:], pool_gain), (sinks[:], sink_cols)):
                pool.dma_start(dst, src).then_inc(const_in, 16)
            pool.dma_start(pool_m, pool_w.rearrange("g (c p) d -> p g c d", p=P)).then_inc(const_in, 16)
            pool.wait_ge(slab_done, SLABS * (N_OUT + 1))
            pool.dma_start(bias, b_qkv.partition_broadcast(P)).then_inc(mixer_in, 16)
            pool.dma_start(bo, b_o.partition_broadcast(P)).then_inc(mixer_in, 16)
            pool.wait_ge(mixer_in, 32)
            pool.wait_ge(rstd_done, 3)
            pool.wait_ge(t_free, T_QKV + 2)
            for t in range(TT):
                last = pool.tensor_tensor(xs[:, t, :], xs[:, t, :], bo, ALU.add)
            last.then_inc(bo_added, 1)
            pool.wait_ge(post_done, posts(N_WO - 1))
            pool.dma_start(fin_gain, final_gain.partition_broadcast(P)).then_inc(final_in, 16)

        @block.tensor
        def _(pe):
            def products(m, part_, s, x_hi, x_lo, tiles):
                for k in range(SK):
                    kt = part_ * SK + k
                    for t in tiles:
                        tok = slice(t * P, (t + 1) * P)
                        hi, lo = w_hi[:, s % RING, k, :], w_lo[:, s % RING, k, :]
                        pe.matmul(acc_of(m, t), x_hi[:, kt, tok], hi, start=(kt == 0), stop=False)
                        pe.matmul(acc_of(m, t), x_hi[:, kt, tok], lo, start=False, stop=False)
                        mm = pe.matmul(acc_of(m, t), x_lo[:, kt, tok], hi, start=False, stop=(kt == KT - 1))
                return mm

            def group(n, x_hi, x_lo, after, before={}, order=None):
                for s in range(SLABS):
                    if s in before:
                        before[s]()
                    m, part_ = (n, s) if order is None else order[s]
                    if part_ == 0 and (not isinstance(m, int) or m >= 2):
                        pe.wait_ge(evac_done, m - 1)
                    pe.wait_ge(lo_done, SLABS * n + s + 1)
                    products(m, part_, s, x_hi, x_lo, range(TT)).then_inc(slab_done, 1)
                    if s in after:
                        after[s]()

            def transposes(T, src, ready, value):
                pe.wait_ge(ready, value)
                if not isinstance(T, int) or T > 0:
                    pe.wait_ge(t_free, T)
                for k in range(4):
                    for t in range(TT):
                        c = (k % 2) * S + t * P
                        mm = pe.transpose(tb[k // 2][:, c:c + P], src(k, t), ident)
                    if k % 2:
                        mm.then_inc(t_full, 1)

            def z_tile(k, t):
                return z[:, t, k * P:(k + 1) * P]

            def zr_tile(k, t):
                return zr[:, t, k * P:(k + 1) * P]

            def z_post(n, T):
                return {1: lambda: transposes(T, z_tile, post_done, posts(n - 1))}

            def x_quarter(j):
                return lambda: transposes(2 * j, lambda k, t: xs[:, t, (4 * j + k) * P:(4 * j + k + 1) * P], x_in[j], 16)

            def x_split(j):
                return lambda: pe.wait_ge(t_free, j + 1)

            pe.wait_ge(first_in, 16)
            x_quarter(0)()
            group(0, a_hi, a_lo, {2 * j - 2: x_quarter(j) for j in range(1, G4)}, {j: x_split(j) for j in range(SLABS)})
            pe.wait_ge(const_in, 16 * 6)

            T, U, head = T_IN, 0, 0

            def rot_post(n, T):
                return {2: lambda: transposes(T, zr_tile, post_done, posts(n - 1))}

            def scores(h2, U, kq_ready):
                pe.wait_ge(t_free, kq_ready)
                if U:
                    pe.wait_ge(aux_free, U)
                for i in range(2):
                    h = 2 * h2 + i
                    pe.matmul(aux[i][:, 0:S], r_kT[:, h, 0:P], r_qT[:, h, :], start=True, stop=True)
                    pe.matmul(aux[i][:, S:S + P], r_kT[:, h, P:S], r_qT[:, h, P:S],
                              start=True, stop=True).then_inc(aux_full, 1)

            def values(h2, head):
                for i in range(2):
                    h = 2 * h2 + i
                    pe.wait_ge(p_done, head + i + 1)
                    v = [z[:, t, h * DK:(h + 1) * DK] for t in range(TT)]
                    o = [tb[t][:, h * DK:(h + 1) * DK] for t in range(TT)]
                    pe.matmul(o[0], r_p[:, i, 0:P], v[0], start=True, stop=True)
                    pe.matmul(o[1], r_p[:, i, P:S], v[0], start=True, stop=False)
                    mm = pe.matmul(o[1], r_p[:, i, S:S + P], v[1], start=False, stop=True)
                    if h < 3:
                        mm.then_inc(p_used, 1)
                    else:
                        mm.then_inc(t_full, 2)

            def retention(n, T, U, head):
                def first():
                    scores(0, U, T)

                def second():
                    pe.wait_ge(evac_done, n)
                    values(0, head)
                    scores(1, U + 2, T)

                def third():
                    values(1, head + 2)
                return {0: first, 2: second, 4: third}

            def pooling(n, T, U):
                def differences():
                    pe.wait_ge(evac_done, n)
                    if U:
                        pe.wait_ge(aux_free, U)
                    for c in range(4):
                        g = 2 * (n - 7) + c // 2
                        d = aux[c // 2][:, (c % 2) * S:(c % 2 + 1) * S]
                        z0, z1 = z_tile(c, 0), z_tile(c, 1)
                        pe.matmul(d[:, 0:P], z0, window[:, g, 0:P], start=True, stop=True)
                        pe.matmul(d[:, P:S], z1, window[:, g, P:2 * P], start=True, stop=True)
                        mm = pe.matmul(d[:, P:P + TAIL], z0, window[:, g, 2 * P:2 * P + TAIL],
                                       start=False, stop=True, skip_group_check=True)
                        if c % 2:
                            mm.then_inc(aux_full, 1)

                def mapped():
                    pe.wait_ge(aux_free, U + 2)
                    pe.wait_ge(t_free, T)
                    for a in range(2):
                        g = 2 * (n - 7) + a
                        for d in range(2):
                            for c in range(2):
                                mm = pe.matmul(tb[a][:, d * S:(d + 1) * S], pool_m[:, g, c, d * P:(d + 1) * P],
                                               diffT[:, 2 * a + c, :], start=(c == 0), stop=(c == 1))
                        mm.then_inc(t_full, 1)
                return {1: differences, 3: mapped}

            for n in range(1, N_IN):
                if n in (1, 2, 4, 5):
                    after = rot_post(n, T)
                    T += 2
                elif n in (3, 6):
                    after = retention(n, T, U, head)
                    T, U, head = T + 2, U + 4, head + 4
                elif n in (7, 8):
                    after = pooling(n, T, U)
                    T, U = T + 2, U + 2
                else:
                    after = z_post(n, T)
                    T += 2
                group(n, a_hi, a_lo, after)

            def need(T):
                return {6: lambda: pe.wait_ge(t_free, T)}

            def wide(n0, x_hi, x_lo, T, first=0):
                with pe.Fori(first, G4 - 1) as i:
                    group(i + (n0 + 1), x_hi, x_lo, z_post(i + (n0 + 1), i * 2 + T))

            group(N_OUT, b_hi, b_lo, z_post(N_OUT, T), need(T + 2))
            T += 2
            wide(N_OUT, b_hi, b_lo, T)
            T += 6

            def mlp(n0, T0):
                group(n0, a_hi, a_lo, z_post(n0, T0), need(T0 + 2))
                T1 = T0 + 2
                with pe.Fori(0, 3) as q:
                    with pe.Fori(0, 3) as i:
                        n = q * 8 + i + (n0 + 1)
                        group(n, a_hi, a_lo, z_post(n, q * 8 + i * 2 + T1))
                    n, T = q * 8 + (n0 + 4), q * 8 + (T1 + 6)
                    group(n, b_hi, b_lo, z_post(n, T), need(T + 2))
                    with pe.Fori(0, 3) as i:
                        group(q * 8 + i + (n0 + 5), b_hi, b_lo, {})
                    group(q * 8 + (n0 + 8), a_hi, a_lo, {})
                n1, T2 = n0 + 24, T1 + 24
                wide(n1, a_hi, a_lo, T2)
                group(n1 + 4, b_hi, b_lo, z_post(n1 + 4, T2 + 6), need(T2 + 8))
                return n1 + 4, T2 + 8

            n1, T = mlp(N_MLP0, T)
            wide(n1, b_hi, b_lo, T)
            T += 6

            group(N_QKV, a_hi, a_lo, z_post(N_QKV, T), need(T + 2))
            T += 2

            def attention(n, g, T, U):
                def scores(two):
                    pe.wait_ge(aux_free, U + 2 * two)
                    for side in range(2):
                        rows_ = slice(side * HD, (side + 1) * HD)
                        for a in range(2):
                            for c in range(2):
                                chunk = 2 * two + c
                                win = (0, 0, 1, 2)[chunk]
                                o = (2 * a + c) * P
                                mm = pe.matmul(aux[side][:, o:o + P], a_qT[rows_, 4 * a + chunk, :],
                                               a_kT[rows_, g, win, :], start=True, stop=True)
                        mm.then_inc(aux_full, 1)

                def probs(two):
                    T1 = T + 2 + 3 * two
                    pe.wait_ge(t_free, T1)
                    pe.wait_ge(prob_done, 2 * g + two + 1)
                    for side in range(2):
                        for i in range(4):
                            mm = pe.transpose(tb[side][:, i * P:(i + 1) * P], e_buf[:, 8 * two + 4 * side + i, 0:P], ident)
                        mm.then_inc(t_full, 1)

                def values(two):
                    T1 = T + 4 + 3 * two
                    pe.wait_ge(t_free, T1)
                    for c in range(2):
                        chunk = 2 * two + c
                        win = (0, 0, 1, 2)[chunk]
                        o = tb[0].rearrange("p (k t) -> p k t", k=4)[:, :, c * CHUNK:(c + 1) * CHUNK]
                        for side in range(2):
                            v = v_pad[:, win * KV + g, (1 - side) * HD:(1 - side) * HD + P]
                            pr = probT[:, 4 * side:4 * side + 4, :].rearrange("p (a c) r -> p a c r", c=2)[:, :, c, :]
                            mm = pe.matmul(o, v, pr, start=(side == 0), stop=(side == 1))
                    mm.then_inc(t_full, 1)

                def run(*steps):
                    return lambda: [f(i) for f, i in steps]

                def queries():
                    transposes(T, z_tile, post_done, posts(n - 1))

                def scores0():
                    pe.wait_ge(t_free, T + 2)
                    scores(0)
                return {1: [queries], 2: [scores0], 4: [run((scores, 1))], 5: [run((probs, 0))],
                        6: [run((values, 0))], 7: [run((probs, 1))]}, {0: [run((values, 1))]}

            group(N_QKV + 1, a_hi, a_lo, {2: lambda: transposes(T, zr_tile, post_done, posts(N_QKV))})
            T += 2
            U = U_ATT
            late = {}
            for g in range(KV):
                n = N_QKV + 2 + g
                steps, later = attention(n, g, T, U)
                after = {s: (lambda fs: lambda: [f() for f in fs])(late.get(s, []) + steps.get(s, [])) for s in range(SLABS)}
                late = later
                if n < N_WO:
                    group(n, a_hi, a_lo, after)
                else:
                    group(n, b_hi, b_lo, after, order=WO_ORDER[:SLABS])
                T, U = T + 8, U + 4

            after = {0: lambda fs=late[0]: [f() for f in fs],
                     WO_DONE: lambda T=T: transposes(T, z_tile, post_done, posts(N_WO))}
            group(N_WO + 1, b_hi, b_lo, after, {WO_DONE - 2: lambda T=T: pe.wait_ge(t_free, T)}, WO_ORDER[SLABS:])
            wide(N_WO, b_hi, b_lo, T, first=1)
            n1, T = mlp(N_MLP1, T + 6)
            with pe.Fori(0, G4 - 2) as i:
                group(i + (n1 + 1), b_hi, b_lo, {})
            n = N_END - 1
            pe.wait_ge(evac_done, n - 1)
            for s in range(SLABS - RING):
                pe.wait_ge(lo_done, SLABS * n + s + 1)
                products(n, s, s, b_hi, b_lo, range(TT)).then_inc(slab_done, 1)
            for s in range(SLABS - RING, SLABS):
                pe.wait_ge(lo_done, SLABS * n + s + 1)
                mm = products(n, s, s, b_hi, b_lo, [0])
            mm.then_inc(tile_done, 1)
            for s in range(SLABS - RING, SLABS):
                products(n, s, s, b_hi, b_lo, [1]).then_inc(slab_done, 1)

        @block.scalar
        def _(act):
            def group(n, after):
                for s in range(SLABS):
                    act.wait_ge(raw_in[s], (n + 1) * 16)
                    if not isinstance(n, int) or n > 0 or s >= RING:
                        act.wait_ge(slab_done, SLABS * n + (s + 1 - RING))
                    act.copy(w_hi[:, s % RING, :, :], raw[:, s, :, :]).then_inc(hi_done, 1)
                    if s in after:
                        for f in after[s]:
                            f()

            def evac(n, func=ACT.Copy, norm=None, slabs=0):
                def run():
                    act.wait_ge(slab_done, SLABS * n + slabs)
                    if norm is not None:
                        act.wait_ge(rstd_done, norm + 1)
                    if not isinstance(n, int) or n >= 2:
                        act.wait_ge(post_done, posts(n - 2))
                    for t in range(TT):
                        s = 1.0 if norm is None else rstd[:, norm, t:t + 1]
                        last = act.activation(z[:, t, :], acc_of(n - 1, t), func, scale=s)
                    last.then_inc(evac_done, 1)
                return run

            def split(T, H, hi, kt, scales=None, banks=(0, 1)):
                def run():
                    for b in banks:
                        act.wait_ge(t_full, T + b + 1)
                        if scales is None:
                            last = act.copy(rows(hi, kt + 2 * b, 2), tb[b].rearrange("p (k t) -> p k t", k=2))
                        else:
                            for k in range(2):
                                last = act.activation(rows(hi, kt + 2 * b + k, 1), tb[b][:, k * S:(k + 1) * S]
                                                      .rearrange("p (k t) -> p k t", k=1), ACT.Identity,
                                                      scale=scales(2 * b + k))
                        last.then_inc(op_hi, 1)
                return run

            def squares(norm, g, src, ready, value):
                def run():
                    for t in range(TT):
                        act.drain()
                        if t == 0:
                            act.wait_ge(ready, value)
                        s = t * G4 + g
                        s = sumsq[:, norm, s:s + 1] if isinstance(s, int) else sumsq[:, norm, bass.ds(s, 1)]
                        last = act.activation(junk[:], src(t), ACT.Square, accum_out=s)
                    act.drain().then_inc(sumsq_done, 1)
                return run

            def root(norm):
                def run():
                    act.wait_ge(mean_done, norm + 1)
                    act.activation(rms[:, norm, :], meansq[:, norm, :], ACT.Sqrt).then_inc(rms_done, 1)
                return run

            act.dma_start(ident_gain[:], ident_gains).then_inc(first_in, 16)
            act.wait_ge(warm, 1)
            act.activation(rms[:, 0, :], rms[:, 0, :], ACT.Identity)
            act.wait_ge(first_in, 16)
            split(0, 0, a_hi, 0, gain_of(0, 0), banks=[0])()
            T, H = T_IN, H_IN

            def copies(T, dst):
                def run():
                    for b in range(2):
                        act.wait_ge(t_full, T + b + 1)
                        act.copy(dst[:, 2 * b:2 * b + 2, :], tb[b].rearrange("p (k t) -> p k t", k=2)) \
                           .then_inc(t_free, 1)
                return run

            def results(T, half):
                def run():
                    act.wait_ge(t_full, T + 2)
                    for t in range(TT):
                        act.copy(r_o[:, t, half * COLS:(half + 1) * COLS], tb[t][:]).then_inc(t_free, 1)
                    act.drain().then_inc(o_out, 1)
                return run

            def deviations(half):
                def run():
                    act.wait_ge(o_centred, half + 1)
                    for t in range(TT):
                        last = act.activation(diffT[:, 2 * t:2 * t + 2, :].rearrange("p a b -> p (a b)"),
                                              r_o[:, t, half * COLS:(half + 1) * COLS], ACT.Square)
                    last.then_inc(o_square, 1)
                return run

            def o_root(half):
                def run():
                    act.wait_ge(o_var, half + 1)
                    act.activation(stat[:, 2, :], stat[:, 1, :], ACT.Sqrt).then_inc(o_std, 1)
                return run

            def differences(U):
                def run():
                    for b in range(2):
                        act.wait_ge(aux_full, U + b + 1)
                        act.copy(diffT[:, 2 * b:2 * b + 2, :], aux[b].rearrange("p (k t) -> p k t", k=2)) \
                           .then_inc(aux_free, 1)
                return run

            U = 0
            for n in range(N_IN):
                after = {}
                if n == 0:
                    after = {2 * j + 1: [split(2 * j, 2 * j, a_hi, 4 * j, gain_of(0, j))] for j in range(1, G4)}
                    after[0] = [split(0, 0, a_hi, 0, gain_of(0, 0), banks=[1])]
                    for g, slot in enumerate((2, 4, 5, 6)):
                        after[slot] = after.get(slot, []) + [
                            squares(0, g, lambda t, g=g: xs[:, t, g * COLS:(g + 1) * COLS], x_in[g], 16)]
                elif n in (1, 2, 4, 5):
                    after = {2: [evac(n, ACT.Identity, 0)], 5: [copies(T, r_qT if n in (1, 4) else r_kT)]}
                    T += 2
                    if n == 1:
                        after[0] = [root(0)]
                    if n == 4:
                        after[3] = [deviations(0)]
                        after[6] = [o_root(0)]
                elif n in (3, 6):
                    after = {2: [evac(n, ACT.Identity, 0)], 7: [results(T, n // 6)]}
                    T, U = T + 2, U + 4
                elif n in (7, 8):
                    after = {2: [evac(n, ACT.Identity, 0)], 4: [differences(U)],
                             6: [split(T, H, b_hi, 4 * (n - 7), pool_gain_of(n - 7))]}
                    if n == 7:
                        after[1] = [deviations(1)]
                        after[3] = [o_root(1)]
                    T, H, U = T + 2, H + 2, U + 2
                elif n == 9:
                    after = {2: [evac(n, ACT.Silu, 0)], 4: [split(T, H, b_hi, 8)]}
                    T, H = T + 2, H + 2
                group(n, after)

            group(N_OUT, {2: [evac(N_OUT, ACT.Silu, 0)], 4: [split(T, H, b_hi, 12)]})
            T, H = T + 2, H + 2

            def x_post(n, norm, layer, g, T, H):
                return {2: [evac(n)],
                        3: [squares(norm, g, lambda t: z[:, t, :], post_done, posts(n - 1))],
                        4: [split(T, H, a_hi, g * 4, gain_of(layer, g))]}

            def x_posts(n0, norm, layer, T, H, first=0):
                with act.Fori(first, 3) as i:
                    group(i + (n0 + 1), x_post(i + (n0 + 1), norm, layer, i, i * 2 + T, i * 2 + H))

            def last_x_post(n, norm, layer, T, H):
                after = x_post(n, norm, layer, 3, T, H)
                after[7] = [root(norm)]
                return after

            def f_post(n, norm, g, T, H):
                return {2: [evac(n, ACT.Relu, norm)], 4: [split(T, H, b_hi, g * 4)]}

            def mlp(n0, norm, layer, next_norm, T, H):
                group(n0, last_x_post(n0, norm, layer, T, H))
                T, H = T + 2, H + 2
                with act.Fori(0, 3) as q:
                    with act.Fori(0, 3) as i:
                        n = q * 8 + i + (n0 + 1)
                        group(n, f_post(n, norm, i, q * 8 + i * 2 + T, q * 8 + i * 2 + H))
                    n = q * 8 + (n0 + 4)
                    group(n, f_post(n, norm, 3, q * 8 + (T + 6), q * 8 + (H + 6)))
                    with act.Fori(0, 3) as i:
                        n = q * 8 + i + (n0 + 5)
                        group(n, {2: [evac(n)]})
                    n = q * 8 + (n0 + 8)
                    group(n, {2: [evac(n)]})
                n1, T, H = n0 + 24, T + 24, H + 24
                with act.Fori(0, 3) as i:
                    n = i + (n1 + 1)
                    group(n, f_post(n, norm, i, i * 2 + T, i * 2 + H))
                group(n1 + 4, f_post(n1 + 4, norm, 3, T + 6, H + 6))
                return n1 + 4, T + 8, H + 8

            x_posts(N_OUT, 1, 1, T, H)
            T, H = T + 6, H + 6
            n1, T, H = mlp(N_MLP0, 1, 1, 2, T, H)
            x_posts(n1, 2, 2, T, H)
            T, H = T + 6, H + 6

            group(N_QKV, last_x_post(N_QKV, 2, 2, T, H))
            T, H = T + 2, H + 2

            def keys(T):
                def run():
                    for b in range(2):
                        act.wait_ge(t_full, T + b + 1)
                        src = tb[b].rearrange("p (g t) -> p g t", g=2)
                        dst = a_kT[:, 2 * b:2 * b + 2, :, :]
                        act.copy(dst[:, :, 0, :], src[:, :, 0:P])
                        act.copy(dst[:, :, 2, :], src[:, :, P:S])
                        act.copy(dst[:, :, 1, 0:CHUNK], src[:, :, 2 * CHUNK:3 * CHUNK])
                        act.copy(dst[:, :, 1, CHUNK:P], src[:, :, CHUNK:2 * CHUNK])
                        act.drain().then_inc(t_free, 1)
                return run

            group(N_QKV + 1, {2: [evac(N_QKV + 1, ACT.Identity, 2)], 5: [keys(T)]})
            T += 2

            def attention(n, g, T, H):
                def queries():
                    for b in range(2):
                        act.wait_ge(t_full, T + b + 1)
                        act.mul(a_qT[:, 4 * b:4 * b + 4, :].rearrange("p c (k q) -> p k c q", k=2),
                                tb[b].rearrange("p (k c q) -> p k c q", k=2, c=4), HD ** -0.5).then_inc(t_free, 1)

                def exps(two):
                    act.wait_ge(max_done, 2 * g + two + 1)
                    act.activation(soft[:, two, 2, :], soft[:, two, 2, :], ACT.Exp)
                    for i in range(8):
                        last = act.activation(e_buf[:, 8 * two + i, :], aux_both[:, i * P:(i + 1) * P], ACT.Exp,
                                              bias=soft[:, two, 1, i:i + 1], accum_out=soft[:, two, 3, i:i + 1])
                    last.then_inc(aux_free, 2)
                    act.drain().then_inc(exp_done, 1)

                def probs(two):
                    for side in range(2):
                        act.wait_ge(t_full, T + 2 + 3 * two + side + 1)
                        act.copy(probT[:, 4 * side:4 * side + 4, :], tb[side].rearrange("p (k t) -> p k t", k=4)) \
                           .then_inc(t_free, 1)

                def result(two):
                    act.wait_ge(t_full, T + 4 + 3 * two + 1)
                    act.copy(b_hi[:, 4 * g:4 * g + 4, two * P:(two + 1) * P],
                             tb[0].rearrange("p (k t) -> p k t", k=4)).then_inc(op_hi, 1)
                return {2: [evac(n, ACT.Identity, 2)], 4: [queries], 6: [lambda: exps(0)]}, \
                    {0: [lambda: probs(0), lambda: exps(1)], 1: [lambda: result(0)], 2: [lambda: probs(1)],
                     3: [lambda: result(1)]}

            late = {}
            for g in range(KV):
                n = N_QKV + 2 + g
                steps, later = attention(n, g, T, H)
                group(n, {s: late.get(s, []) + steps.get(s, []) for s in range(SLABS)})
                T, H, late = T + 8, H + 2, later

            def wo_post(n):
                return {WO_DONE + 2: [evac(n, slabs=WO_DONE)],
                        WO_DONE + 3: [squares(3, 0, lambda t: z[:, t, :], post_done, posts(n - 1)),
                                      split(T, H, a_hi, 0, gain_of(3, 0))]}
            group(N_WO + 1, {**late, **wo_post(N_WO + 1)})
            x_posts(N_WO, 3, 3, T, H, first=1)
            T, H = T + 6, H + 6
            n1, T, H = mlp(N_MLP1, 3, 3, 4, T, H)
            with act.Fori(0, 3) as i:
                n = i + (n1 + 1)
                group(n, {2: [evac(n)], 3: [squares(4, i, lambda t: z[:, t, :], post_done, posts(n - 1))]})
            for t in range(TT):
                act.wait_ge(post_done, posts(N_END - 1) + t)
                act.drain()
                act.activation(junk[:], z[:, t, :], ACT.Square, accum_out=sumsq[:, 4, t * G4 + 3:t * G4 + 4])
                act.drain().then_inc(sumsq_done, 1)
                act.wait_ge(mean_done, 4 + t + 1)
                act.activation(rms[:, 4, t:t + 1], meansq[:, 4, t:t + 1], ACT.Sqrt).then_inc(rms_done, 1)
                act.wait_ge(rstd_done, 4 + t + 1)
                for g in (1, 2):
                    xg = xs[:, t, g * COLS:(g + 1) * COLS]
                    act.activation(xg, xg, ACT.Copy, scale=rstd[:, 4, t:t + 1]).then_inc(out_act, 1)

        @block.vector
        def _(dve):
            def group(n, after):
                for s in range(SLABS):
                    dve.wait_ge(hi_done, SLABS * n + (s + 1))
                    dve.tensor_tensor(w_lo[:, s % RING, :, :], raw[:, s, :, :],
                                      w_hi[:, s % RING, :, :].bitcast(F32), ALU.subtract).then_inc(lo_done, 1)
                    if s in after:
                        for f in after[s]:
                            f()

            def split(H, hi, lo, kt, scales=None, banks=(0, 1)):
                def run():
                    for b in banks:
                        dve.wait_ge(op_hi, H + b + 1)
                        if scales is None:
                            last = dve.tensor_tensor(rows(lo, kt + 2 * b, 2), tb[b].rearrange("p (k t) -> p k t", k=2),
                                                     rows(hi, kt + 2 * b, 2).bitcast(F32), ALU.subtract)
                        else:
                            for k in range(2):
                                last = dve.scalar_tensor_tensor(
                                    out=rows(lo, kt + 2 * b + k, 1),
                                    in0=tb[b][:, k * S:(k + 1) * S].rearrange("p (k t) -> p k t", k=1),
                                    scalar=scales(2 * b + k), in1=rows(hi, kt + 2 * b + k, 1).bitcast(F32),
                                    op0=ALU.mult, op1=ALU.subtract)
                        last.then_inc(t_free, 1)
                return run

            def mean(norm):
                def run():
                    dve.wait_ge(sumsq_done, G4 * (norm + 1))
                    dve.tensor_reduce(meansq[:, norm, :], sumsq[:, norm, :].rearrange("p (t g) -> p t g", g=G4),
                                      AX_X, ALU.add)
                    dve.drain()
                    dve.tensor_scalar(meansq[:, norm, :], meansq[:, norm, :], 1.0 / D, EPS, ALU.mult, ALU.add) \
                       .then_inc(mean_done, 1)
                return run

            def inverse(norm):
                def run():
                    dve.wait_ge(rms_done, norm + 1)
                    dve.reciprocal(rstd[:, norm, :], rms[:, norm, :]).then_inc(rstd_done, 1)
                return run

            dve.memset(rms[:, 0, :], 0.0).then_inc(warm, 1)
            dve.wait_ge(first_in, 16)
            split(0, a_hi, a_lo, 0, gain_of(0, 0), banks=[0])()
            H = H_IN

            def rotate(n):
                def run():
                    dve.wait_ge(evac_done, n)
                    half = DK // 2
                    src = [z[:].rearrange("p t (h d) -> p t h d", h=4)[:, :, :, i * half:(i + 1) * half] for i in (0, 1)]
                    dst = [zr[:].rearrange("p t (h d) -> p t h d", h=4)[:, :, :, i * half:(i + 1) * half] for i in (0, 1)]
                    cos, sin = (trig[:, :, i, :].unsqueeze(2).broadcast_to([P, TT, 4, half]) for i in (0, 1))
                    dve.tensor_tensor(dst[0], src[0], cos, ALU.mult)
                    dve.tensor_tensor(rot, src[1], sin, ALU.mult)
                    dve.tensor_tensor(dst[1], src[0], sin, ALU.mult)
                    dve.drain()
                    dve.tensor_tensor(dst[0], dst[0], rot, ALU.subtract)
                    dve.drain()
                    dve.tensor_tensor(rot, src[1], cos, ALU.mult)
                    dve.drain()
                    dve.tensor_tensor(dst[1], dst[1], rot, ALU.add)
                    dve.drain().then_inc(post_done, 1)
                return run

            def decays(half, h2, U):
                def run():
                    for i in range(2):
                        h = 4 * half + 2 * h2 + i
                        dve.wait_ge(aux_full, U + i + 1)
                        if h2 == 1:
                            dve.wait_ge(p_used, 3 * half + i + 1)
                        dve.tensor_tensor(r_p[:, i, 0:S], aux[i][:, 0:S], decay[:, h, :], ALU.mult)
                        dve.tensor_tensor(r_p[:, i, S:S + P], aux[i][:, S:S + P], decay[:, h, 0:P], ALU.mult) \
                           .then_inc(aux_free, 1)
                        dve.drain().then_inc(p_done, 1)
                return run

            def heads_of(half):
                o = r_o[:, :, half * COLS:(half + 1) * COLS].rearrange("p t (h d) -> p t h d", h=4)
                return o

            def per_head(i):
                return stat[:, i, :].rearrange("p (t h) -> p t h", t=TT)

            def centre(half):
                def run():
                    o = heads_of(half)
                    dve.wait_ge(o_out, half + 1)
                    dve.tensor_reduce(per_head(0), o, AX_X, ALU.add)
                    dve.drain()
                    dve.tensor_scalar(stat[:, 0, :], stat[:, 0, :], 1.0 / DK, None, ALU.mult)
                    dve.drain()
                    dve.tensor_tensor(o, o, per_head(0).unsqueeze(3).broadcast_to([P, TT, 4, DK]), ALU.subtract) \
                       .then_inc(o_centred, 1)
                return run

            def variance(half):
                def run():
                    dve.wait_ge(o_square, half + 1)
                    dve.tensor_reduce(stat[:, 1, :], diffT.rearrange("p a (h d) -> p (a h) d", h=2), AX_X, ALU.add)
                    dve.drain()
                    dve.tensor_scalar(stat[:, 1, :], stat[:, 1, :], 1.0 / DK, EPS, ALU.mult, ALU.add) \
                       .then_inc(o_var, 1)
                return run

            def scale(half):
                def run():
                    o = heads_of(half)
                    dve.wait_ge(o_std, half + 1)
                    dve.reciprocal(stat[:, 3, :], stat[:, 2, :])
                    dve.drain()
                    dve.tensor_tensor(o, o, per_head(3).unsqueeze(3).broadcast_to([P, TT, 4, DK]), ALU.mult)
                return run

            def gate(n, half):
                def run():
                    dve.wait_ge(evac_done, n)
                    dve.drain()
                    dve.tensor_tensor(z[:], z[:], r_o[:, :, half * COLS:(half + 1) * COLS], ALU.mult) \
                       .then_inc(post_done, 1)
                return run

            U = 0
            for n in range(N_IN):
                after = {}
                if n == 0:
                    after = {2 * j + 1: [split(2 * j, a_hi, a_lo, 4 * j, gain_of(0, j))] for j in range(1, G4)}
                    after[0] = [split(0, a_hi, a_lo, 0, gain_of(0, 0), banks=[1])]
                elif n in (1, 2, 4, 5):
                    after = {2: [rotate(n)]}
                    if n == 1:
                        after[0] = [mean(0), lambda: dve.wait_ge(const_in, 16 * 6)]
                        after[1] = [inverse(0)]
                    if n == 4:
                        after[1] = [centre(0)]
                        after[4] = [variance(0)]
                        after[7] = [scale(0)]
                elif n in (3, 6):
                    after = {3: [decays(n // 6, 0, U)], 5: [decays(n // 6, 1, U + 2)]}
                    U += 4
                elif n in (7, 8):
                    after = {6: [split(H, b_hi, b_lo, 4 * (n - 7), pool_gain_of(n - 7))]}
                    if n == 7:
                        after[0] = [centre(1)]
                        after[2] = [variance(1)]
                        after[4] = [scale(1)]
                    H += 2
                elif n == 9:
                    after = {2: [gate(n, 0)], 4: [split(H, b_hi, b_lo, 8)]}
                    H += 2
                group(n, after)

            group(N_OUT, {2: [gate(N_OUT, 1)], 4: [split(H, b_hi, b_lo, 12)]})
            H += 2

            def x_add(n, g, keep):
                def run():
                    dve.wait_ge(evac_done, n)
                    xg = cols(xs, g * COLS, COLS)
                    add = dve.tensor_tensor(xg, xg, z[:], ALU.add)
                    if not keep:
                        add.then_inc(post_done, 1)
                        return
                    dve.drain()
                    dve.tensor_copy(z[:], xg).then_inc(post_done, 1)
                return run

            def x_post(n, layer, g, H):
                return {2: [x_add(n, g, True)], 4: [split(H, a_hi, a_lo, g * 4, gain_of(layer, g))]}

            def x_posts(n0, layer, H, first=0):
                with dve.Fori(first, 3) as i:
                    group(i + (n0 + 1), x_post(i + (n0 + 1), layer, i, i * 2 + H))

            def last_x_post(n, norm, layer, H):
                after = x_post(n, layer, 3, H)
                after[6] = [mean(norm)]
                after[7] = [inverse(norm)]
                return after

            def f_post(n, g, H):
                def square():
                    dve.wait_ge(evac_done, n)
                    dve.tensor_tensor(z[:], z[:], z[:], ALU.mult).then_inc(post_done, 1)
                return {2: [square], 4: [split(H, b_hi, b_lo, g * 4)]}

            def mlp(n0, norm, layer, H):
                group(n0, last_x_post(n0, norm, layer, H))
                H += 2
                with dve.Fori(0, 3) as q:
                    with dve.Fori(0, 3) as i:
                        n = q * 8 + i + (n0 + 1)
                        group(n, f_post(n, i, q * 8 + i * 2 + H))
                    n = q * 8 + (n0 + 4)
                    group(n, f_post(n, 3, q * 8 + (H + 6)))
                    with dve.Fori(0, 3) as i:
                        n = q * 8 + i + (n0 + 5)
                        group(n, {2: [x_add(n, i, False)]})
                    n = q * 8 + (n0 + 8)
                    group(n, {2: [x_add(n, 3, False)]})
                n1, H = n0 + 24, H + 24
                with dve.Fori(0, 3) as i:
                    n = i + (n1 + 1)
                    group(n, f_post(n, i, i * 2 + H))
                group(n1 + 4, f_post(n1 + 4, 3, H + 6))
                return n1 + 4, H + 8

            x_posts(N_OUT, 1, H)
            H += 6
            n1, H = mlp(N_MLP0, 1, 1, H)
            x_posts(n1, 2, H)
            H += 6

            def zeros():
                dve.memset(v_pad, 0.0)
                dve.tensor_scalar(minus_sinks[:], sinks[:], -1.0, None, ALU.mult)
            after = last_x_post(N_QKV, 2, 2, H)
            after[1] = [zeros]
            group(N_QKV, after)
            H += 2

            def keys_values():
                dve.wait_ge(evac_done, N_QKV + 1)
                dve.wait_ge(mixer_in, 32)
                kd = zr[:].rearrange("p t (g u d) -> p t g u d", g=KV, u=2)
                for t in range(TT):
                    k = z[:, t, 0:KV * HD].rearrange("p (g d) -> p g d", g=KV)
                    for u in range(2):
                        dve.tensor_tensor(kd[:, t, :, u, :], k, bias[:, D:D + 256].rearrange("p (g d) -> p g d", g=KV),
                                          ALU.add)
                vb = bias[:, D + 256:D + 512].rearrange("p (g d) -> p g d", g=KV)
                for win, t, lo, hi in ((0, 0, 0, P), (2, 1, 0, P), (1, 1, 0, CHUNK), (1, 0, CHUNK, P)):
                    v = z[lo:hi, t, 256:512].rearrange("p (g d) -> p g d", g=KV)
                    last = dve.tensor_tensor(v_pad[lo:hi, win * KV:(win + 1) * KV, HD:2 * HD], v, vb[lo:hi], ALU.add)
                dve.drain().then_inc(post_done, 1)

            group(N_QKV + 1, {2: [keys_values]})

            def attention(n, g, H):
                def queries():
                    dve.wait_ge(evac_done, n)
                    b = bias[:, g * COLS:(g + 1) * COLS].unsqueeze(1).broadcast_to([P, TT, COLS])
                    dve.tensor_tensor(z[:], z[:], b, ALU.add).then_inc(post_done, 1)

                def maxima(two):
                    scores = aux_both.rearrange("p (k l) -> p k l", k=8)
                    top, minus_m, sink_term = (soft[:, two, i, :] for i in range(3))
                    dve.wait_ge(aux_full, U_ATT + 4 * g + 2 * two + 2)
                    if two == 0:
                        dve.memset(scores.rearrange("p (a c) l -> p a c l", c=2)[:, :, 0, CHUNK:P], NEG_INF)
                        dve.drain()
                    dve.tensor_reduce(top, scores, AX_X, ALU.max)
                    dve.drain()
                    per_chunk = [v[:, 4 * g:4 * g + 4].unsqueeze(2).broadcast_to([P, 4, 2]) for v in (sinks, minus_sinks)]
                    top, minus_m, sink_term = (v.rearrange("p (a c) -> p a c", c=2) for v in (top, minus_m, sink_term))
                    dve.scalar_tensor_tensor(out=minus_m, in0=top, scalar=-1.0, in1=per_chunk[1],
                                             op0=ALU.mult, op1=ALU.min)
                    dve.drain()
                    dve.tensor_tensor(sink_term, minus_m, per_chunk[0], ALU.add).then_inc(max_done, 1)

                def probabilities(two):
                    e = e_buf[:, 8 * two:8 * two + 8, :]
                    sink_term, total, inv = (soft[:, two, i, :] for i in (2, 3, 4))
                    dve.wait_ge(exp_done, 2 * g + two + 1)
                    dve.tensor_tensor(total, total, sink_term, ALU.add)
                    dve.drain()
                    dve.reciprocal(inv, total)
                    dve.drain()
                    dve.tensor_tensor(e, e, inv.unsqueeze(2).broadcast_to([P, 8, P]), ALU.mult).then_inc(prob_done, 1)

                def result(two):
                    dve.wait_ge(op_hi, H + two + 1)
                    tok = slice(two * P, (two + 1) * P)
                    dve.tensor_tensor(b_lo[:, 4 * g:4 * g + 4, tok], tb[0].rearrange("p (k t) -> p k t", k=4),
                                      b_hi[:, 4 * g:4 * g + 4, tok].bitcast(F32), ALU.subtract).then_inc(t_free, 1)
                def run(f, two):
                    return lambda: f(two)
                return {2: [queries], 5: [run(maxima, 0)], 7: [run(probabilities, 0), run(maxima, 1)]}, \
                    {0: [run(probabilities, 1)], 1: [run(result, 0)], 3: [run(result, 1)]}

            late = {}
            for g in range(KV):
                n = N_QKV + 2 + g
                steps, later = attention(n, g, H)
                group(n, {s: late.get(s, []) + steps.get(s, []) for s in range(SLABS)})
                H, late = H + 2, later

            dve.wait_ge(bo_added, 1)
            group(N_WO + 1, {**late, WO_DONE + 2: [x_add(N_WO + 1, 0, True)],
                             WO_DONE + 3: [split(H, a_hi, a_lo, 0, gain_of(3, 0))]})
            x_posts(N_WO, 3, H, first=1)
            H += 6
            n1, H = mlp(N_MLP1, 3, 3, H)
            dve.wait_ge(final_in, 16)

            def x_final(n, g):
                def run():
                    dve.wait_ge(evac_done, n)
                    xg = cols(xs, g * COLS, COLS)
                    dve.tensor_tensor(z[:], z[:], xg, ALU.add).then_inc(post_done, 1)
                    dve.wait_ge(post_done, posts(n - 1))
                    fg = fin_gain[:, bass.ds(g * COLS, COLS)] if not isinstance(g, int) else fin_gain[:, g * COLS:]
                    dve.tensor_tensor(xg, z[:], fg.unsqueeze(1).broadcast_to([P, TT, COLS]), ALU.mult)
                return run

            with dve.Fori(0, 3) as i:
                group(i + (n1 + 1), {2: [x_final(i + (n1 + 1), i)]})
            dve.wait_ge(sumsq_done, G4 * 4 + 3)
            for t, (done, value) in enumerate(((tile_done, 1), (slab_done, SLABS * N_END))):
                dve.wait_ge(done, value)
                dve.tensor_tensor(z[:, t, :], acc_of(N_END - 1, t), xs[:, t, D - COLS:], ALU.add).then_inc(post_done, 1)
                dve.wait_ge(sumsq_done, G4 * 4 + 3 + t + 1)
                mean_t = meansq[:, 4, t:t + 1]
                dve.tensor_reduce(mean_t, sumsq[:, 4, t * G4:(t + 1) * G4], AX_X, ALU.add)
                dve.drain()
                dve.tensor_scalar(mean_t, mean_t, 1.0 / D, EPS, ALU.mult, ALU.add).then_inc(mean_done, 1)
                dve.wait_ge(rms_done, 4 + t + 1)
                rstd_t = rstd[:, 4, t:t + 1]
                dve.reciprocal(rstd_t, rms[:, 4, t:t + 1]).then_inc(rstd_done, 1)
                dve.drain()
                dve.tensor_scalar(xs[:, t, 0:COLS], xs[:, t, 0:COLS], rstd_t, None, ALU.mult).then_inc(out_dve, 1)
                dve.scalar_tensor_tensor(out=xs[:, t, D - COLS:], in0=z[:, t, :], scalar=rstd_t, in1=fin_gain[:, D - COLS:],
                                         op0=ALU.mult, op1=ALU.mult).then_inc(out_dve, 1)


def rotary_table():
    half = DK // 2
    inv_freq = (np.float32(10000.0) ** (-np.arange(half, dtype=np.float32) / np.float32(half))).astype(np.float32)
    ang = np.arange(S, dtype=np.float32)[:, None] * inv_freq[None, :]
    t = np.stack([np.cos(ang), np.sin(ang)], axis=1)
    return np.ascontiguousarray(t.reshape(TT, P, 2, half).transpose(1, 0, 2, 3).astype(np.float32))


def decay_table():
    g = 1.0 - 2.0 ** (-5.0 - np.arange(HEADS))[:, None, None]
    j, i = np.arange(P)[:, None], np.arange(P)[None, :]
    same = np.where(j // CHUNK <= i // CHUNK, g ** np.abs(i - j), 0.0)
    later = g ** (P + i - j)
    t = np.concatenate([same, later], axis=2) * DK ** -0.5
    return np.ascontiguousarray(t.transpose(1, 0, 2).astype(np.float32))


def window_table():
    s, t = np.arange(S)[:, None], np.arange(S)[None, :]
    out = np.zeros((P, len(POOL_WINDOWS), 2 * P + TAIL))
    for g, w in enumerate(POOL_WINDOWS):
        m = np.where((s <= t) & (s > t - w), 1.0 / np.minimum(t + 1, w), 0.0) - (s == t)
        out[:, g, 0:P], out[:, g, P:2 * P], out[:, g, 2 * P:] = m[:P, :P], m[P:, P:], m[:P, P:P + TAIL]
    return out.astype(np.float32)


def kernel(x, mix_norm, mlp_norm, w1, w2, rp_w_in, pool_w, pool_scale, rp_w_out,
           attn_w_qkv, attn_b_qkv, attn_sinks, attn_w_o, attn_b_o, final_norm):
    import concourse.bacc as _bacc
    from concourse.bass_utils import run_bass_kernel_spmd as _run

    a = {k: np.asarray(v) for k, v in dict(
        x=x, mix_norm=mix_norm, mlp_norm=mlp_norm, w1=w1, w2=w2, w_in=rp_w_in, pool_w=pool_w,
        pool_scale=pool_scale, w_out=rp_w_out, w_qkv=attn_w_qkv, b_qkv=attn_b_qkv, sinks=attn_sinks,
        w_o=attn_w_o, b_o=attn_b_o, final=final_norm).items()}
    norms = np.stack([a["mix_norm"][0], a["mlp_norm"][0], a["mix_norm"][1], a["mlp_norm"][1]])
    gains = norms.reshape(4, KT, P).transpose(2, 0, 1).reshape(P, 4 * KT)
    ident_gains = np.concatenate([np.eye(P, dtype=np.float32), gains], axis=1)
    pool_gain = np.ascontiguousarray(a["pool_scale"][0].reshape(8, P).T)
    s = a["sinks"][0].reshape(KV, 2, 2, 2).transpose(2, 0, 3, 1).reshape(2, 4 * KV)
    sink_cols = np.ascontiguousarray(np.repeat(s, HD, axis=0))
    arrays = {
        "x": a["x"][0], "ident_gains": ident_gains, "w1": a["w1"], "w2": a["w2"], "w_in": a["w_in"][0],
        "pool_w": a["pool_w"][0], "pool_gain": pool_gain, "w_out": a["w_out"][0], "w_qkv": a["w_qkv"][0],
        "b_qkv": a["b_qkv"][0], "sink_cols": sink_cols, "w_o": a["w_o"][0], "b_o": a["b_o"][0],
        "final_gain": a["final"], "rotary_c": rotary_table(),
        "decay_c": decay_table(), "window_c": window_table(),
    }
    arrays = {k: np.ascontiguousarray(v) for k, v in arrays.items()}
    nc = _bacc.Bacc("TRN2", target_bir_lowering=False, num_devices=1)
    args = {k: nc.dram_tensor(f"in_{k}", v.shape, mybir.dt.from_np(v.dtype), kind="ExternalInput").ap()
            for k, v in arrays.items()}
    out = nc.dram_tensor("out_0", (S, D), F32, kind="ExternalOutput").ap()
    build_program(nc, out=out, **args)
    r = _run(nc, [{f"in_{k}": v for k, v in arrays.items()}], core_ids=[0])
    return r.results[0]["out_0"].reshape(1, S, D)
```
